# Optimizing a Trainium2 kernel written in Bass

```python
import jax, jax.numpy as jnp
from jax import lax
import numpy as np

D_MODEL = 1024
BATCH = 1
SEQ = 256
DEPTH = 1
DEC_BATCH = 1
DEC_SEQ = 1024
PAST_LEN = 128

GRID_W = 64
NA_HEADS = 8
NA_HEAD_DIM = 64
NA_WIDTH = NA_HEADS * NA_HEAD_DIM
NA_KH_MAX = 8
NA_KW = 16
HG_HEADS = 4
HG_HEAD_DIM = 128
HG_WIDTH = HG_HEADS * HG_HEAD_DIM
HG_CHUNK = 64
N_EXPERTS = 16
EC_FACTOR = 2
D_FF = 2 * D_MODEL
IN_WIDTH = 3 * NA_WIDTH + 5 * HG_WIDTH + 2 * D_MODEL
ALPHA = (2 * DEPTH) ** 0.25
BETA = (8 * DEPTH) ** -0.25
LN_EPS = 1e-5
RMS_EPS = 1e-6
NEG_BIG = -1e30
F_MIN = 1e-30

kernel_name = 'hybrid_na_hgrn2_ec_encoder'

def layer_norm(x, g, b):
    xf = x.astype(jnp.float32)
    mu = jnp.mean(xf, axis=-1, keepdims=True)
    var = jnp.mean(jnp.square(xf - mu), axis=-1, keepdims=True)
    return ((xf - mu) * lax.rsqrt(var + LN_EPS)).astype(x.dtype) * g + b

def neighbourhood_attention(q, k, v, rpb):
    B, T, H, dh = q.shape
    rows = T // GRID_W
    kh = min(NA_KH_MAX, rows)
    r = jnp.arange(rows)
    row_idx = jnp.clip(r - kh // 2, 0, rows - kh)[:, None] + jnp.arange(kh)[None, :]
    c = jnp.arange(GRID_W)
    c_start = jnp.clip(c - NA_KW // 2, 0, GRID_W - NA_KW)
    col_mask = (c[None, :] >= c_start[:, None]) & (c[None, :] < c_start[:, None] + NA_KW)
    dr = row_idx - r[:, None] + (NA_KH_MAX - 1)
    dc = jnp.clip(c[None, :] - c[:, None], -(NA_KW - 1), NA_KW - 1) + (NA_KW - 1)
    bias = rpb[:, dr[:, None, :, None], dc[None, :, None, :]].astype(jnp.float32)
    bias = jnp.where(col_mask[None, None, :, None, :], bias, NEG_BIG)
    scale = dh ** -0.5

    def one(args):
        qb, kb, vb = args
        qg = qb.reshape(rows, GRID_W, H, dh)
        kg = kb.reshape(rows, GRID_W, H, dh)[row_idx]
        vg = vb.reshape(rows, GRID_W, H, dh)[row_idx]
        s = jnp.einsum('rqhd,rjkhd->hrqjk', qg, kg, preferred_element_type=jnp.float32) * scale + bias
        p = jax.nn.softmax(s.reshape(H, rows, GRID_W, kh * GRID_W), axis=-1)
        p = p.reshape(s.shape).astype(vb.dtype)
        o = jnp.einsum('hrqjk,rjkhd->rqhd', p, vg)
        return o.reshape(T, H, dh)

    return lax.map(one, (q, k, v))

def lower_bounds(p):
    sm = jax.nn.softmax(p.astype(jnp.float32), axis=0)
    return jnp.cumsum(sm, axis=0) - sm[0:1]

def forget_gates(z, lb):
    z = z.astype(jnp.float32)
    f = lb + (1.0 - lb) * jax.nn.sigmoid(z)
    log_f = jnp.log(jnp.maximum(f, F_MIN))
    k = (1.0 - lb) * jax.nn.sigmoid(-z)
    return k, log_f

def hgrn2_chunk_scan(q, k, v, log_f):
    B, T, H, dk = q.shape
    dv = v.shape[-1]
    n = T // HG_CHUNK

    def chunks(a):
        return a.reshape(B, n, HG_CHUNK, H, a.shape[-1]).transpose(1, 0, 3, 2, 4)

    tri = jnp.tril(jnp.ones((HG_CHUNK, HG_CHUNK), dtype=bool))

    def step(S, inp):
        qc, kc, vc, gc = inp
        b = jnp.cumsum(gc, axis=2)
        o_inter = jnp.einsum('bhtk,bhkv->bhtv', qc * jnp.exp(b), S)
        diff = jnp.where(tri[:, :, None], b[:, :, :, None, :] - b[:, :, None, :, :], NEG_BIG)
        a = jnp.einsum('bhtk,bhsk,bhtsk->bhts', qc, kc, jnp.exp(diff))
        o = o_inter + jnp.einsum('bhts,bhsv->bhtv', a, vc)
        b_last = b[:, :, -1]
        S = jnp.exp(b_last)[..., None] * S + jnp.einsum('bhsk,bhsv->bhkv', kc * jnp.exp(b_last[:, :, None] - b), vc)
        return S, o

    S0 = jnp.zeros((B, H, dk, dv), jnp.float32)
    _, o = lax.scan(step, S0, (chunks(q), chunks(k), chunks(v), chunks(log_f)))
    return o.transpose(1, 0, 3, 2, 4).reshape(B, T, H, dv)

def hgrn2_bidirectional(q, i, z_fwd, z_bwd, lb_fwd, lb_bwd):
    q = q.astype(jnp.float32)
    v = i.astype(jnp.float32)
    k_f, g_f = forget_gates(z_fwd, lb_fwd)
    k_b, g_b = forget_gates(z_bwd, lb_bwd)
    o_f = hgrn2_chunk_scan(q, k_f, v, g_f)
    flip = lambda a: jnp.flip(a, axis=1)
    o_b = flip(hgrn2_chunk_scan(flip(q), flip(k_b), flip(v), flip(g_b)))
    return o_f + o_b

def rms_norm_heads(o, g):
    B, T, H, dv = o.shape
    o = o * lax.rsqrt(jnp.mean(jnp.square(o), axis=-1, keepdims=True) + RMS_EPS)
    return o.reshape(B, T, H * dv) * g.astype(jnp.float32)

def expert_choice_ffn(x, w_router, w_gate, w_up, w_down):
    B, T, D = x.shape
    n_tok = B * T
    cap = EC_FACTOR * n_tok // N_EXPERTS
    xf = x.reshape(n_tok, D)
    aff = jax.nn.softmax((xf @ w_router).astype(jnp.float32), axis=-1)
    gate, idx = lax.top_k(aff.T, cap)
    xs = xf[idx]
    hdn = jax.nn.silu(jnp.einsum('ecd,edf->ecf', xs, w_gate)) * jnp.einsum('ecd,edf->ecf', xs, w_up)
    out = jnp.einsum('ecf,efd->ecd', hdn, w_down) * gate[..., None].astype(x.dtype)
    y = jnp.zeros_like(xf).at[idx.reshape(-1)].add(out.reshape(-1, D))
    return y.reshape(B, T, D)

def trunk(x, ln_in_g, ln_in_b, w_in, na_rpb, hg_lb_fwd, hg_lb_bwd, hg_norm_g,
          w_branch_na, w_branch_hg, w_out, ln1_g, ln1_b, w_router,
          w_gate_e, w_up_e, w_down_e, ln2_g, ln2_b):
    B, T, _ = x.shape
    lb_fwd = lower_bounds(hg_lb_fwd)
    lb_bwd = lower_bounds(hg_lb_bwd)
    sizes = [NA_WIDTH] * 3 + [HG_WIDTH] * 5 + [D_MODEL]
    splits = [int(s) for s in np.cumsum(sizes)]
    heads_na = lambda a: a.reshape(B, T, NA_HEADS, NA_HEAD_DIM)
    heads_hg = lambda a: a.reshape(B, T, HG_HEADS, HG_HEAD_DIM)
    x = layer_norm(x, ln_in_g, ln_in_b)
    for l in range(DEPTH):
        h = x @ w_in[l]
        q_na, k_na, v_na, q_hg, z_f, z_b, i_hg, g_hg, gate_na, gate_hg = jnp.split(h, splits, axis=-1)
        a_out = neighbourhood_attention(heads_na(q_na), heads_na(k_na), heads_na(v_na), na_rpb[l])
        a_out = a_out.reshape(B, T, NA_WIDTH) @ w_branch_na[l]
        o_hg = hgrn2_bidirectional(heads_hg(jax.nn.silu(q_hg)), heads_hg(i_hg), heads_hg(z_f), heads_hg(z_b),
                                   lb_fwd[l].reshape(HG_HEADS, HG_HEAD_DIM),
                                   lb_bwd[l].reshape(HG_HEADS, HG_HEAD_DIM))
        o_hg = rms_norm_heads(o_hg, hg_norm_g[l]).astype(x.dtype)
        r_out = (o_hg * jax.nn.silu(g_hg)) @ w_branch_hg[l]
        mix = jax.nn.sigmoid(gate_na) * a_out + jax.nn.sigmoid(gate_hg) * r_out
        x = layer_norm(ALPHA * x + mix @ w_out[l], ln1_g[l], ln1_b[l])
        y = expert_choice_ffn(x, w_router[l], w_gate_e[l], w_up_e[l], w_down_e[l])
        x = layer_norm(ALPHA * x + y, ln2_g[l], ln2_b[l])
    return x

def setup_inputs(seed: int = 0) -> dict:
    key = jax.random.key(seed)
    ks = jax.random.split(key, 21)
    nrm = lambda k, shape, s: jax.random.normal(k, shape, jnp.float32) * s
    return {
        'x_prompt': nrm(ks[0], (BATCH, SEQ, D_MODEL), 1.0),
        'x_sample': nrm(ks[1], (DEC_BATCH, DEC_SEQ, D_MODEL), 1.0),
        'ln_in_g': 1.0 + nrm(ks[2], (D_MODEL,), 0.02),
        'ln_in_b': nrm(ks[3], (D_MODEL,), 0.02),
        'w_in': nrm(ks[4], (DEPTH, D_MODEL, IN_WIDTH), D_MODEL ** -0.5),
        'na_rpb': nrm(ks[5], (DEPTH, NA_HEADS, 2 * NA_KH_MAX - 1, 2 * NA_KW - 1), 0.1),
        'hg_lb_fwd': nrm(ks[6], (DEPTH, HG_WIDTH), 0.1),
        'hg_lb_bwd': nrm(ks[7], (DEPTH, HG_WIDTH), 0.1),
        'hg_norm_g': 1.0 + nrm(ks[8], (DEPTH, HG_WIDTH), 0.02),
        'w_branch_na': nrm(ks[9], (DEPTH, NA_WIDTH, D_MODEL), NA_WIDTH ** -0.5),
        'w_branch_hg': nrm(ks[10], (DEPTH, HG_WIDTH, D_MODEL), HG_WIDTH ** -0.5),
        'w_out': nrm(ks[11], (DEPTH, D_MODEL, D_MODEL), BETA * D_MODEL ** -0.5),
        'ln1_g': 1.0 + nrm(ks[12], (DEPTH, D_MODEL), 0.02),
        'ln1_b': nrm(ks[13], (DEPTH, D_MODEL), 0.02),
        'w_router': nrm(ks[14], (DEPTH, D_MODEL, N_EXPERTS), D_MODEL ** -0.5),
        'w_gate_e': nrm(ks[15], (DEPTH, N_EXPERTS, D_MODEL, D_FF), D_MODEL ** -0.5),
        'w_up_e': nrm(ks[16], (DEPTH, N_EXPERTS, D_MODEL, D_FF), D_MODEL ** -0.5),
        'w_down_e': nrm(ks[17], (DEPTH, N_EXPERTS, D_FF, D_MODEL), BETA * D_FF ** -0.5),
        'ln2_g': 1.0 + nrm(ks[18], (DEPTH, D_MODEL), 0.02),
        'ln2_b': nrm(ks[19], (DEPTH, D_MODEL), 0.02),
    }

def reference(x_prompt, x_sample, ln_in_g, ln_in_b, w_in, na_rpb, hg_lb_fwd, hg_lb_bwd, hg_norm_g,
              w_branch_na, w_branch_hg, w_out, ln1_g, ln1_b, w_router,
              w_gate_e, w_up_e, w_down_e, ln2_g, ln2_b):
    y_prompt = trunk(x_prompt, ln_in_g, ln_in_b, w_in, na_rpb, hg_lb_fwd, hg_lb_bwd, hg_norm_g,
                     w_branch_na, w_branch_hg, w_out, ln1_g, ln1_b, w_router,
                     w_gate_e, w_up_e, w_down_e, ln2_g, ln2_b)
    y_sample = trunk(x_sample, ln_in_g, ln_in_b, w_in, na_rpb, hg_lb_fwd, hg_lb_bwd, hg_norm_g,
                     w_branch_na, w_branch_hg, w_out, ln1_g, ln1_b, w_router,
                     w_gate_e, w_up_e, w_down_e, ln2_g, ln2_b)
    return (y_prompt, y_sample)


_drawn_inputs = setup_inputs


def setup_inputs(seed=0):
    import zlib

    import numpy as np

    out = dict(_drawn_inputs(seed))
    spreads = {}
    factors = {'ln_in_b': 2.685,
     'na_rpb': 8.0,
     'hg_norm_g': 8.0,
     'ln1_g': 2.685,
     'ln2_g': 8.401,
     'ln2_b': 8.245,
     'ln1_b': 3.423}
    for name, (base, spread) in spreads.items():
        noise = np.random.default_rng([zlib.crc32(name.encode()), seed]).standard_normal(out[name].shape)
        drawn = base * np.exp(spread * noise) if base else spread * noise
        out[name] = __import__('jax').numpy.asarray(drawn.astype(out[name].dtype))
    for name, factor in factors.items():
        out[name] = (out[name] * factor).astype(out[name].dtype)
    return out
```

```python
import math
from contextlib import ExitStack

import concourse.bass as bass
from concourse import mybir

F32 = mybir.dt.float32
F32R = mybir.dt.float32r
I32 = mybir.dt.int32
U32 = mybir.dt.uint32
U8 = mybir.dt.uint8
ACT = mybir.ActivationFunctionType
ALU = mybir.AluOpType
AX = mybir.AxisListType

P = 128
D = 1024
KD = D // P
SEQS = ((0, 256), (256, 1024))
T = 1280
NT = T // P
GRID_W = 64
NA_HEADS, NA_DIM = 8, 64
KH, KW = 8, 16
HG_HEADS = 4
NAW = NA_HEADS * NA_DIM
HGW = HG_HEADS * P
IN_W = 3 * NAW + 5 * HGW + 2 * D
COL_Q, COL_K, COL_V = 0, NAW, 2 * NAW
COL_HQ, COL_ZF, COL_ZB, COL_I, COL_G = (3 * NAW + n * HGW for n in range(5))
COL_GATE = 3 * NAW + 5 * HGW
NE = 16
CAPS = (2 * 256 // NE, 2 * 1024 // NE)
TOK = CAPS[0] + CAPS[1]
FF = 2 * D
NFT = FF // P
ALPHA = 2 ** 0.25
LN_EPS, RMS_EPS = 1e-5, 1e-6
NEG_BIG = -1e30
F_MIN = 1e-30
SLAB = 512
NSLAB = IN_W // SLAB


class Steps:

    def __init__(self, per):
        self.per, self.base, self.n = per, 0, 0

    def round(self, r):
        assert self.n in (0, self.per), (self.n, self.per)
        self.base, self.n = r * self.per, 0

    def next(self):
        self.n += 1
        return self.base + self.n


class Stage:

    def __init__(self, nc, ctx, name):
        self.nc, self.ctx, self.name = nc, ctx, name
        self.semaphores = []
        ctx.callback(self.release)

    def sb(self, name, shape, dt=F32):
        return self.ctx.enter_context(self.nc.sbuf_tensor(f"{self.name}_{name}", shape, dt))

    def ps(self, name, shape, dt=F32):
        return self.ctx.enter_context(self.nc.psum_tensor(f"{self.name}_{name}", shape, dt))

    def sem(self, name):
        self.semaphores.append(self.nc.alloc_semaphore(f"{self.name}_{name}"))
        return self.semaphores[-1]

    def sems(self, name, n):
        return [self.sem(f"{name}{i}") for i in range(n)]

    def release(self):
        if self.semaphores:
            self.nc.clear_and_free_semaphores(self.semaphores)
            self.nc.all_engine_barrier()


def held(eng, count):
    return count if isinstance(count, int) else eng.to_reg(count)


def in_steps(eng, parts):
    last = max(lag for lag, _ in parts)

    def step(i, u):
        for lag, part in parts:
            if not isinstance(i, int) or 0 <= 2 * i + u - lag < NT:
                part(2 * i + u - lag, (u - lag) % 2, i + (u - lag) // 2)

    first = (last + 1) // 2
    for n in range(2 * first):
        step(n // 2, n % 2)
    with eng.Fori(first, NT // 2) as i:
        for u in range(2):
            step(i, u)
    for n in range(NT, NT + last):
        step(n // 2, n % 2)


def rows_of(vector_ap, n):
    return bass.AP(vector_ap.tensor, offset=vector_ap.offset, ap=[[0, P], [1, n]])


def stage_consts(nc, ident):
    with ExitStack() as ctx:
        s = Stage(nc, ctx, "const")
        zeroed, made = s.sem("zeroed"), s.sem("made")
        with nc.Block() as block:
            @block.gpsimd
            def _(pool):
                nc.gpsimd.memset(ident[:], 0.0).then_inc(zeroed, 1)
                pool.wait_ge(zeroed, 1)
                nc.gpsimd.affine_select(out=ident[:], in_=ident[:], compare_op=ALU.not_equal, fill=1.0,
                                        base=0, pattern=[[-1, P]], channel_multiplier=1).then_inc(made, 1)
                pool.wait_ge(made, 1)


def stage_norm_in(nc, ident, x, g, b, xln, xT_hi, xT_lo):
    with ExitStack() as ctx:
        s = Stage(nc, ctx, "ln0")
        x_in = s.sb("x_in", [P, 2, D])
        y = s.sb("y", [P, 2, D])
        g_all, b_all = s.sb("g_all", [P, D]), s.sb("b_all", [P, D])
        stats, mv = s.sb("stats", [P, 2, 6]), s.sb("mv", [P, 2])
        rstd, veps, minus_half = s.sb("rstd", [P, 1]), s.sb("veps", [P, 1]), s.sb("mhalf", [P, 1])
        tp = [s.ps(f"tp{u}", [P, D]) for u in range(2)]
        consts_in = s.sem("consts_in")
        x_ready, x_read = s.sems("x_ready", 2), s.sems("x_read", 2)
        half_made, var_eps = s.sem("half_made"), s.sem("var_eps")
        var_ready, rstd_ready = s.sem("var_ready"), s.sem("rstd_ready")
        chain, y_ready = s.sem("chain"), s.sems("y_ready", 2)
        y_stored, y_turned = s.sems("y_stored", 2), s.sems("y_turned", 2)
        hi_done, lo_done = s.sem("hi_done"), s.sems("lo_done", 2)
        with nc.Block() as block:
            @block.sync
            def _(sp):
                sp.dma_start(g_all[:], rows_of(g, D)).then_inc(consts_in, 16)
                sp.dma_start(b_all[:], rows_of(b, D)).then_inc(consts_in, 16)
                with sp.Fori(0, NT // 2) as i:
                    for u in range(2):
                        sp.wait_ge(x_read[u], i)
                        sp.dma_start(x_in[:, u, :], x[bass.ds((2 * i + u) * P, P), :]).then_inc(x_ready[u], 16)

            @block.vector
            def _(dve):
                dve.wait_ge(consts_in, 32)
                step = Steps(8)
                with dve.Fori(0, NT // 2) as i:
                    step.round(i)
                    for u in range(2):
                        t = 2 * i + u
                        dve.wait_ge(x_ready[u], 16 * i + 16)
                        nc.vector.bn_stats(stats[:, 0, :], x_in[:, u, 0:512]).then_inc(chain, 1)
                        step.next()
                        nc.vector.bn_stats(stats[:, 1, :], x_in[:, u, 512:1024]).then_inc(chain, 1)
                        count = held(dve, step.next())
                        dve.wait_ge(consts_in, 32)
                        dve.wait_ge(chain, count)
                        nc.vector.bn_aggr(mv[:], stats[:]).then_inc(var_ready, 1)
                        dve.wait_ge(y_stored[u], 16 * i)
                        dve.wait_ge(y_turned[u], i)
                        dve.wait_ge(var_ready, t + 1)
                        dve.wait_ge(rstd_ready, t + 1)
                        nc.vector.tensor_scalar(y[:, u, :], x_in[:, u, :], mv[:, 0:1], rstd[:], ALU.subtract,
                                                ALU.mult).then_inc(x_read[u], 1)
                        dve.wait_ge(x_read[u], i + 1)
                        nc.vector.tensor_tensor(y[:, u, :], y[:, u, :], g_all[:], ALU.mult).then_inc(chain, 1)
                        dve.wait_ge(chain, step.next())
                        nc.vector.tensor_tensor(y[:, u, :], y[:, u, :], b_all[:], ALU.add).then_inc(y_ready[u], 1)
                        dve.wait_ge(hi_done, t + 1)
                        for h in range(2):
                            lo = nc.vector.tensor_tensor(
                                xT_lo[:, 4 * h:4 * h + 4, bass.ds(t * P, P)],
                                tp[u][:, 512 * h:512 * h + 512].rearrange("p (k c) -> p k c", k=4),
                                xT_hi[:, 4 * h:4 * h + 4, bass.ds(t * P, P)].bitcast(F32), ALU.subtract)
                            if h == 0:
                                lo.then_inc(chain, 1)
                                step.next()
                        lo.then_inc(lo_done[u], 1)

            @block.gpsimd
            def _(pool):
                nc.gpsimd.memset(minus_half[:], -0.5).then_inc(half_made, 1)
                pool.wait_ge(half_made, 1)
                with pool.Fori(0, NT // 2) as i:
                    for u in range(2):
                        t = 2 * i + u
                        count = held(pool, t + 1)
                        pool.wait_ge(half_made, 1)
                        pool.wait_ge(var_ready, count)
                        nc.gpsimd.tensor_scalar(veps[:], mv[:, 1:2], LN_EPS, None, ALU.add).then_inc(var_eps, 1)
                        pool.wait_ge(var_eps, t + 1)
                        nc.gpsimd.tensor_tensor(rstd[:], veps[:], minus_half[:], ALU.pow).then_inc(rstd_ready, 1)
                        count = held(pool, i + 1)
                        pool.wait_ge(half_made, 1)
                        pool.wait_ge(y_ready[u], count)
                        pool.dma_start(xln[bass.ds(t * P, P), :], y[:, u, :]).then_inc(y_stored[u], 16)
                for u in range(2):
                    pool.wait_ge(y_stored[u], 16 * (NT // 2))

            @block.tensor
            def _(pe):
                with pe.Fori(0, NT // 2) as i:
                    for u in range(2):
                        pe.wait_ge(y_ready[u], i + 1)
                        pe.wait_ge(lo_done[u], i)
                        for k in range(KD):
                            last = nc.tensor.transpose(tp[u][:, k * P:(k + 1) * P], y[:, u, k * P:(k + 1) * P],
                                                       ident[:])
                        last.then_inc(y_turned[u], 1)

            @block.scalar
            def _(act):
                with act.Fori(0, NT // 2) as i:
                    for u in range(2):
                        t = 2 * i + u
                        act.wait_ge(y_turned[u], i + 1)
                        for h in range(2):
                            last = nc.scalar.activation(
                                xT_hi[:, 4 * h:4 * h + 4, bass.ds(t * P, P)],
                                tp[u][:, 512 * h:512 * h + 512].rearrange("p (k c) -> p k c", k=4), ACT.Copy)
                        last.then_inc(hi_done, 1)


def stage_project(nc, w_in, h, xT_hi, xT_lo, bias_on_pool):
    NB = 5
    with ExitStack() as ctx:
        s = Stage(nc, ctx, "proj")
        raw = s.sb("raw", [P, 2, 4, SLAB])
        w_hi, w_lo = s.sb("w_hi", [P, 2, KD, SLAB], F32R), s.sb("w_lo", [P, 2, KD, SLAB], F32R)
        out = s.sb("out", [P, NB, SLAB])
        acc = [s.ps(f"acc{n}", [P, SLAB]) for n in range(NB)]
        w_ready, hi_done, lo_done = s.sems("w_ready", 2), s.sems("hi_done", 2), s.sems("lo_done", 2)
        mm_done, slab_done = s.sems("mm_done", NB), s.sems("slab_done", 2)
        copied, stored = s.sems("copied", NB), s.sems("stored", NB)
        w_view = w_in.rearrange("(k p) n -> p k n", p=P)
        with nc.Block() as block:
            @block.gpsimd
            def _(pool):
                for part in bias_on_pool:
                    part(pool)

            @block.sync
            def _(sp):
                with sp.Fori(0, NSLAB) as j:
                    for v in range(2):
                        sp.wait_ge(lo_done[v], j)
                        sp.dma_start(raw[:, v], w_view[:, 4 * v:4 * v + 4, bass.ds(j * SLAB, SLAB)])\
                          .then_inc(w_ready[v], 16)

            @block.scalar
            def _(act):
                def split(j, u, uses):
                    act.wait_ge(slab_done[u], uses)
                    for v in range(2):
                        act.wait_ge(w_ready[v], 16 * j + 16)
                        nc.scalar.activation(w_hi[:, u, 4 * v:4 * v + 4, :], raw[:, v], ACT.Copy)\
                          .then_inc(hi_done[v], 1)

                def slab(i, u, last):
                    j = 2 * i + u
                    for t in range(NT):
                        n, r = t % NB, 2 * j + t // NB
                        if t == 4 and not last:
                            split(j + 1, 1 - u, i + u)
                        if t % 2 == 0:
                            act.wait_ge(mm_done[n], j + 1 if n == NB - 1 else r + 1)
                            act.wait_ge(stored[n], 16 * r)
                            nc.scalar.activation(out[:, n, :], acc[n][:], ACT.Copy).then_inc(copied[n], 1)
                        act.wait_ge(copied[n], r + 1)
                        act.dma_start(h[t * P:(t + 1) * P, bass.ds(j * SLAB, SLAB)], out[:, n, :])\
                           .then_inc(stored[n], 16)

                split(0, 0, 0)
                with act.Fori(0, NSLAB // 2 - 1) as i:
                    slab(i, 0, False)
                    slab(i, 1, False)
                slab(NSLAB // 2 - 1, 0, False)
                slab(NSLAB // 2 - 1, 1, True)
                for n in range(NB):
                    act.wait_ge(stored[n], 16 * 2 * NSLAB)

            @block.vector
            def _(dve):
                def split(j, u):
                    for v in range(2):
                        dve.wait_ge(hi_done[v], j + 1)
                        nc.vector.tensor_tensor(w_lo[:, u, 4 * v:4 * v + 4, :], raw[:, v],
                                                w_hi[:, u, 4 * v:4 * v + 4, :].bitcast(F32), ALU.subtract)\
                          .then_inc(lo_done[v], 1)

                def slab(i, u, last):
                    j = 2 * i + u
                    for t in range(NT):
                        n, r = t % NB, 2 * j + t // NB
                        if t == 4 and not last:
                            split(j + 1, 1 - u)
                        if t % 2:
                            if t == NT - 1:
                                dve.wait_ge(slab_done[u], i + 1)
                            else:
                                dve.wait_ge(mm_done[n], r + 1)
                            dve.wait_ge(stored[n], 16 * r)
                            nc.vector.tensor_copy(out[:, n, :], acc[n][:]).then_inc(copied[n], 1)

                split(0, 0)
                with dve.Fori(0, NSLAB // 2 - 1) as i:
                    slab(i, 0, False)
                    slab(i, 1, False)
                slab(NSLAB // 2 - 1, 0, False)
                slab(NSLAB // 2 - 1, 1, True)

            @block.tensor
            def _(pe):
                with pe.Fori(0, NSLAB // 2) as i:
                    for u in range(2):
                        j = 2 * i + u
                        for t in range(NT):
                            n, r = t % NB, 2 * j + t // NB
                            pe.wait_ge(copied[n], r)
                            for k in range(KD):
                                if t == 0 and k % 4 == 0:
                                    pe.wait_ge(lo_done[k // 4], j + 1)
                                tile = slice(t * P, (t + 1) * P)
                                nc.tensor.matmul(acc[n][:], xT_hi[:, k, tile], w_hi[:, u, k, :],
                                                 start=(k == 0), stop=False)
                                nc.tensor.matmul(acc[n][:], xT_hi[:, k, tile], w_lo[:, u, k, :],
                                                 start=False, stop=False)
                                last = nc.tensor.matmul(acc[n][:], xT_lo[:, k, tile], w_hi[:, u, k, :],
                                                        start=False, stop=(k == KD - 1))
                            last.then_inc(slab_done[u] if t == NT - 1 else mm_done[n], 1)


NROW = 14


def attention_items():
    items = []
    for first, tokens in SEQS:
        rows = tokens // GRID_W
        kh = min(KH, rows)
        for r0 in range(0, rows, 2):
            s0, s1 = (min(max(r - kh // 2, 0), rows - kh) for r in (r0, r0 + 1))
            assert s0 % 2 == 0 and s1 - s0 in (0, 1)
            items.append(((first + r0 * GRID_W) // P, (first + s0 * GRID_W) // P,
                          (kh + s1 - s0) * GRID_W, s0 - r0 + 6, s1 != s0))
    return items


def bias_pad(nc, rpb, padded, sb, sems):
    zeroed, read, written = sems
    W = 2 * GRID_W - 1
    n = NA_HEADS * (2 * KH - 1)

    def on_pool(pool):
        nc.gpsimd.memset(sb[0:n, :], 0.0).then_inc(zeroed, 1)
        pool.wait_ge(zeroed, 1)
        pool.dma_start(sb[0:n, GRID_W - KW:GRID_W + KW - 1], rpb.rearrange("h r c -> (h r) c")).then_inc(read, 16)
        pool.wait_ge(read, 16)
        pool.dma_start(padded, sb[0:n, :].unsqueeze(1).to_broadcast([n, GRID_W, W])).then_inc(written, 16)
        pool.wait_ge(written, 16)
    return on_pool


def bias_tables(nc, padded, table, sems):
    loaded, masked = sems
    W = 2 * GRID_W - 1

    def on_pool(pool):
        for head in range(NA_HEADS):
            for half in range(2):
                row = head * (2 * KH - 1) + 1 - half
                src = bass.AP(padded, offset=row * GRID_W * W + GRID_W - 1,
                              ap=[[W - 1, GRID_W], [GRID_W * W, NROW], [1, GRID_W]])
                pool.dma_start(table[half * GRID_W:(half + 1) * GRID_W, head], src).then_inc(loaded, 16)
        pool.wait_ge(loaded, 16 * 2 * NA_HEADS)
        w = GRID_W - KW
        n = 0
        for half in range(2):
            rows = table[half * GRID_W:(half + 1) * GRID_W].rearrange("p h n c -> p (h n) c")
            nc.gpsimd.affine_select(out=rows[:, :, 0:w], in_=rows[:, :, 0:w], compare_op=ALU.is_ge, fill=NEG_BIG,
                                    base=KW // 2, pattern=[[0, NA_HEADS * NROW], [1, w]],
                                    channel_multiplier=-1).then_inc(masked, 1)
            n += 1
            pool.wait_ge(masked, n)
            nc.gpsimd.affine_select(out=rows[:, :, KW:], in_=rows[:, :, KW:], compare_op=ALU.is_gt, fill=NEG_BIG,
                                    base=KW // 2 - KW, pattern=[[0, NA_HEADS * NROW], [-1, w]],
                                    channel_multiplier=1).then_inc(masked, 1)
            n += 1
            pool.wait_ge(masked, n)
    return on_pool


def stage_attention(nc, ident, h, table, aT):
    items = [(t, k0, keys, row, two, u) for t, k0, keys, row, two in attention_items() for u in range(2)]
    N = len(items)
    SCALE = NA_DIM ** -0.5
    MAXK = (KH + 1) * GRID_W
    SLOTS = 4
    assert N % SLOTS == 0
    with ExitStack() as ctx:
        s = Stage(nc, ctx, "na")
        qkv = s.sb("qkv", [P, 2, 3, NT, P])
        qz = s.sb("qz", [P, 2, T])
        kT = s.sb("kT", [P, T])
        sc = s.sb("sc", [P, SLOTS, MAXK])
        pT = s.sb("pT", [P, 2, 5 * P])
        out = s.sb("out", [P, 2, T])
        nmax, total, inv = (s.sb(name, [P, SLOTS]) for name in ("nmax", "total", "inv"))
        s_ps = [s.ps(f"s{m}", [P, 2, 512]) for m in range(2)]
        t_ps = s.ps("t", [P, 2 * 512])
        o_ps = [s.ps(f"o{m}", [P, 512]) for m in range(2)]
        loaded, stored, slot_done = s.sems("loaded", 2), s.sems("stored", 2), s.sems("slot_done", 2)
        qz_zeroed, turned, turned_read = s.sem("qz_zeroed"), s.sem("turned"), s.sem("turned_read")
        qk_done, biased, edges, maxed, exp_done = (s.sem(n) for n in ("qk_done", "biased", "edges", "maxed", "exp"))
        inverted, normed, p_turned, p_copied = (s.sem(n) for n in ("inverted", "normed", "p_turned", "p_copied"))
        pv_done, o_copied = s.sem("pv_done"), s.sem("o_copied")
        groups = [(x, a, min(4, NT - a)) for x in range(2) for a in range(0, NT, 4)]
        G = len(groups)
        n_two = sum(it[4] for it in items)
        with nc.Block() as block:
            @block.sync
            def _(sp):
                with sp.Fori(0, 2) as i:
                    for w in range(2):
                        hp = 2 * i + w
                        sp.wait_ge(slot_done[w], i)
                        for x, col in enumerate((COL_Q, COL_K, COL_V)):
                            sp.dma_start(qkv[:, w, x],
                                         h[:, bass.ds(hp * P + col, P)].rearrange("(t p) c -> p t c", p=P))\
                              .then_inc(loaded[w], 16)

            @block.gpsimd
            def _(pool):
                with pool.Fori(0, 2) as i:
                    for w in range(2):
                        hp = 2 * i + w
                        pool.wait_ge(o_copied, (hp + 1) * NT)
                        pool.dma_start(aT[bass.ds(hp * P, P), :], out[:, w]).then_inc(stored[w], 16)
                for w in range(2):
                    pool.wait_ge(stored[w], 32)

            @block.tensor
            def _(pe):
                def scores(g, n, w):
                    t, k0, keys, row, two, u = items[n]
                    if n >= 2:
                        pe.wait_ge(biased, g - 1)
                    half = keys // 2
                    for a in range(2):
                        last = nc.tensor.matmul(s_ps[n % 2][:, a, 0:half], qz[:, u, t * P:(t + 1) * P],
                                                kT[:, k0 * P + a * half:k0 * P + (a + 1) * half],
                                                start=True, stop=True)
                    last.then_inc(qk_done, 1)

                def turn(g, n):
                    keys = items[n][2]
                    pe.wait_ge(normed, g + 1)
                    if n >= 1:
                        pe.wait_ge(p_copied, g)
                    for c in range(0, keys, P):
                        m = min(P, keys - c)
                        last = nc.tensor.transpose(t_ps[0:m, c:c + P], sc[:, n % SLOTS, c:c + m], ident[:])
                    last.then_inc(p_turned, 1)

                def values(g, hp, n, i, w):
                    t, k0, keys, row, two, u = items[n]
                    pe.wait_ge(p_copied, g + 1)
                    if n // 2 >= 2:
                        pe.wait_ge(o_copied, hp * NT + n // 2 - 1)
                    for c in range(0, keys, P):
                        m = min(P, keys - c)
                        last = nc.tensor.matmul(o_ps[(n // 2) % 2][u * 64:u * 64 + 64, 0:P],
                                                qkv[0:m, w, 2, k0 + c // P, u * 64:u * 64 + 64],
                                                pT[0:m, n % 2, c:c + P], start=(c == 0), stop=(c + P >= keys))
                    last.then_inc(slot_done[w] if n == N - 1 else pv_done, 1)

                pe.wait_ge(qz_zeroed, 1)
                with pe.Fori(0, 2) as i:
                    for w in range(2):
                        hp = 2 * i + w
                        pe.wait_ge(loaded[w], 48 * i + 48)
                        for m, (x, a, count) in enumerate(groups):
                            if m >= 2:
                                pe.wait_ge(turned_read, hp * G + m - 1)
                            for c in range(count):
                                last = nc.tensor.transpose(t_ps[:, (m % 2) * 512 + c * P:(m % 2) * 512 + (c + 1) * P],
                                                           qkv[:, w, x, a + c, :], ident[:])
                            last.then_inc(turned, 1)
                        pe.wait_ge(turned_read, hp * G + G)
                        g0 = hp * N
                        for n in range(N + 3):
                            if n < N:
                                scores(g0 + n, n, w)
                            if 2 <= n < N + 2:
                                turn(g0 + n - 2, n - 2)
                            if n >= 3:
                                values(g0 + n - 3, hp, n - 3, i, w)

            @block.vector
            def _(dve):
                def bias(g, hp, n, n_before):
                    t, k0, keys, row, two, u = items[n]
                    half = keys // 2
                    dve.wait_ge(qk_done, g + 1)
                    if n >= SLOTS:
                        dve.wait_ge(p_turned, g - SLOTS + 1)
                    nc.vector.scalar_tensor_tensor(
                        sc[:, n % SLOTS, 0:keys].rearrange("p (a c) -> p a c", a=2), s_ps[n % 2][:, :, 0:half], SCALE,
                        table[:, bass.ds(2 * hp + u, 1), row:row + keys // GRID_W, :]
                        .rearrange("p h n c -> p (h n c)").rearrange("p (a c) -> p a c", a=2),
                        ALU.mult, ALU.add).then_inc(biased, 1)
                    dve.wait_ge(biased, g + 1)
                    if two:
                        nc.vector.memset(sc[0:64, n % SLOTS, KH * GRID_W:keys], NEG_BIG).then_inc(edges, 1)
                        nc.vector.memset(sc[64:128, n % SLOTS, 0:GRID_W], NEG_BIG).then_inc(edges, 1)
                        dve.wait_ge(edges, 2 * (hp * n_two + n_before + 1))
                    nc.vector.tensor_reduce(nmax[:, n % SLOTS:n % SLOTS + 1], sc[:, n % SLOTS, 0:keys], AX.X, ALU.max,
                                            negate=True).then_inc(maxed, 1)

                def norm(g, n):
                    keys = items[n][2]
                    dve.wait_ge(exp_done, g + 1)
                    nc.vector.reciprocal(inv[:, n % SLOTS:n % SLOTS + 1], total[:, n % SLOTS:n % SLOTS + 1]).then_inc(inverted, 1)
                    dve.wait_ge(inverted, g + 1)
                    nc.vector.tensor_scalar(sc[:, n % SLOTS, 0:keys], sc[:, n % SLOTS, 0:keys], inv[:, n % SLOTS:n % SLOTS + 1], None,
                                            ALU.mult).then_inc(normed, 1)

                nc.vector.memset(qz[:], 0.0).then_inc(qz_zeroed, 1)
                with dve.Fori(0, 4) as hp:
                    for n in range(N + 1):
                        if n < N:
                            bias(hp * N + n, hp, n, sum(it[4] for it in items[:n]))
                        if n >= 1:
                            norm(hp * N + n - 1, n - 1)

            @block.scalar
            def _(act):
                def exp(g, n):
                    keys = items[n][2]
                    act.wait_ge(maxed, g + 1)
                    nc.scalar.activation(sc[:, n % SLOTS, 0:keys], sc[:, n % SLOTS, 0:keys], ACT.Exp,
                                         bias=nmax[:, n % SLOTS:n % SLOTS + 1],
                                         accum_out=total[:, n % SLOTS:n % SLOTS + 1]).then_inc(exp_done, 1)

                act.wait_ge(qz_zeroed, 1)
                with act.Fori(0, 2) as i:
                    for w in range(2):
                        hp = 2 * i + w
                        g0 = hp * N
                        for m, (x, a, count) in enumerate(groups):
                            act.wait_ge(turned, hp * G + m + 1)
                            src = t_ps[:, (m % 2) * 512:(m % 2) * 512 + count * P]
                            cols = slice(a * P, (a + count) * P)
                            if x == 0:
                                nc.scalar.activation(qz[0:64, 0, cols], src[0:64], ACT.Copy)
                                last = nc.scalar.activation(qz[64:128, 1, cols], src[64:128], ACT.Copy)
                            else:
                                last = nc.scalar.activation(kT[:, cols], src, ACT.Copy)
                            last.then_inc(turned_read, 1)
                        act.wait_ge(stored[w], 16 * i)
                        for n in range(N + 5):
                            if 3 <= n < N + 3:
                                m = n - 3
                                act.wait_ge(p_turned, g0 + m + 1)
                                if m >= 2:
                                    act.wait_ge(pv_done, hp * (N - 1) + m - 1)
                                keys = items[m][2]
                                full = keys // P * P
                                last = nc.scalar.activation(pT[:, m % 2, 0:full], t_ps[:, 0:full], ACT.Copy)
                                if keys > full:
                                    last = nc.scalar.activation(pT[0:keys - full, m % 2, full:full + P],
                                                                t_ps[0:keys - full, full:full + P], ACT.Copy)
                                last.then_inc(p_copied, 1)
                            if n < N:
                                exp(g0 + n, n)
                            if n >= 5 and n % 2 == 0:
                                m = n - 5
                                if m == N - 1:
                                    act.wait_ge(slot_done[w], i + 1)
                                else:
                                    act.wait_ge(pv_done, hp * (N - 1) + m + 1)
                                t = items[m][0]
                                nc.scalar.activation(out[:, w, t * P:(t + 1) * P], o_ps[(m // 2) % 2][:, 0:P],
                                                     ACT.Copy).then_inc(o_copied, 1)


LEVELS = int(math.log2(P))
CHUNK_GROUPS = [(a, min(4, NT - a)) for a in range(0, NT, 4)]
LN_SPLIT = 2.0 ** -60


def stage_recurrence(nc, ident, h, lb_fwd, lb_bwd, o):
    assert all(first % P == 0 and tokens % P == 0 for first, tokens in SEQS)
    starts = {first // P for first, _ in SEQS}
    ends = {(first + tokens) // P - 1 for first, tokens in SEQS}
    NG = len(CHUNK_GROUPS)
    R = 2 + LEVELS
    NL = 1 + LEVELS
    with ExitStack() as ctx:
        s = Stage(nc, ctx, "hg")
        raw = s.sb("raw", [P, 3, NT, P])
        v = s.sb("v", [P, NT, HGW])
        sgq, qT, ksum = s.sb("sgq", [P, T]), s.sb("qT", [P, T]), s.sb("ksum", [P, T])
        k = s.sb("k", [P, 2, T])
        f, lf = s.sb("f", [P, 2, T]), s.sb("lf", [P, 2, T])
        E = s.sb("E", [P, 2, NT, P + 1])
        W = s.sb("W", [P, 2, 2, T])
        qi = s.sb("qi", [P, 2, T])
        kiT = s.sb("kiT", [P, 2, NT, P])
        decay = s.sb("decay", [P, 2, NT])
        S = s.sb("S", [P, 2, NT, P])
        A = s.sb("A", [P, T])
        out = s.sb("out", [P, NT, P])
        diag = s.sb("diag", [P, 4, P])
        mask = s.sb("mask", [P, LEVELS, 4 * P], U8)
        cols_i, rows_i, xor_i = (s.sb(n, [P, 4 * P], I32) for n in ("cols_i", "rows_i", "xor_i"))
        below = s.sb("below", [P, 4 * P])
        lb, omlb = s.sb("lb", [P, 2, HG_HEADS]), s.sb("omlb", [P, 2, HG_HEADS])
        lb_e, lb_r = s.sb("lb_e", [P, 2, HG_HEADS]), s.sb("lb_r", [P, 2, HG_HEADS])
        tp = [s.ps(f"tp{m}", [P, 512]) for m in range(2)]
        sp_ps = [s.ps(f"s{m}", [P, 512]) for m in range(2)]
        l_ps = [s.ps(f"l{m}", [P, 512]) for m in range(NG)]
        (raw_in, v_in, lb_in, iota_done, in_turned, sg_done, q_read, z_read, clamped, ln_done, scanned, dec_done,
         pool_d, dve_d, exp_done, w_ready, ki_turned, ki_copied, l_mm, a_done, ds_mm, s_made, o_mm, o_copied,
         stored, chain, lb_ready) = (s.sem(n) for n in (
             "raw_in", "v_in", "lb_in", "iota_done", "in_turned", "sg_done", "q_read", "z_read", "clamped", "ln_done",
             "scanned", "dec_done", "pool_d", "dve_d", "exp_done", "w_ready", "ki_turned", "ki_copied", "l_mm",
             "a_done", "ds_mm", "s_made", "o_mm", "o_copied", "stored", "chain", "lb_ready"))
        in_groups = [(x, a, n) for x in range(3) for a, n in CHUNK_GROUPS]
        ki_groups = [(0, a, n) for a, n in CHUNK_GROUPS] + [(1, a, n) for a, n in reversed(CHUNK_GROUPS)]
        made = [sum(c not in (ends, starts)[d] for d, a, n in ki_groups[:m + 1] for c in range(a, a + n))
                for m in range(2 * NG)]
        NS = made[-1]
        e_to = E[:, :, :, 0:P]
        e_with = E[:, :, :, 1:P + 1]

        def halves(view, m, side):
            return view.rearrange("p c (b h j) -> p c b h j", h=2, j=m)[:, :, :, side, :]

        def middle(d, m):
            return E[:, d, :, m:P:2 * m].unsqueeze(3).to_broadcast([P, NT, P // (2 * m), m])

        def chunked(view):
            return view.rearrange("p (c t) -> p c t", t=P)

        def exponents(r):
            z, y = (chunked(W[:, r % 2, x, :]) for x in range(2))
            last = [E[:, d, :, P:P + 1].to_broadcast([P, NT, P]) for d in range(2)]
            if r == 0:
                return [(y, last[0], e_with[:, 0])]
            if r == 1:
                return [(z, last[1], e_to[:, 1])]
            m = P >> (r - 1)
            return [(halves(y, m, 0), middle(0, m), halves(e_with[:, 0], m, 0)),
                    (halves(y, m, 1), halves(e_to[:, 1], m, 1), middle(1, m)),
                    (halves(z, m, 0), middle(1, m), halves(e_to[:, 1], m, 0)),
                    (halves(z, m, 1), halves(e_with[:, 0], m, 1), middle(0, m))]

        def wait_slot(eng, hd, r):
            if r in (2, 3):
                eng.wait_ge(ki_turned, hd * 2 * NG + (r - 1) * NG)
            elif r > 3:
                eng.wait_ge(l_mm, (hd * NL + r - 2) * NG)

        with nc.Block() as block:
            @block.sync
            def _(sp):
                with nc.allow_non_contiguous_dma(reason="512 lower bounds, one per partition and head"):
                    for d, src in enumerate((lb_fwd, lb_bwd)):
                        sp.dma_start(lb[:, d, :], src.rearrange("(h p) -> p h", p=P)).then_inc(lb_in, 16)
                sp.dma_start(v[:], h[:, COL_I:COL_I + HGW].rearrange("(t p) c -> p t c", p=P)).then_inc(v_in, 16)
                with sp.Fori(0, HG_HEADS) as hd:
                    sp.wait_ge(z_read, hd * 2 * NG)
                    for x, col in enumerate((COL_HQ, COL_ZF, COL_ZB)):
                        sp.dma_start(raw[:, x], h[:, bass.ds(hd * P + col, P)].rearrange("(t p) c -> p t c", p=P))\
                          .then_inc(raw_in, 16)
                    count = held(sp, (hd + 1) * NG)
                    sp.wait_ge(v_in, 16)
                    sp.wait_ge(o_copied, count)
                    sp.dma_start(o[:, bass.ds(hd * P, P)].rearrange("(t p) c -> p t c", p=P), out[:])\
                      .then_inc(stored, 16)
                sp.wait_ge(stored, 16 * HG_HEADS)

            @block.gpsimd
            def _(pool):
                nc.gpsimd.iota(cols_i[:], pattern=[[0, 4], [1, P]], base=0, channel_multiplier=0).then_inc(iota_done, 1)
                nc.gpsimd.iota(rows_i[:], pattern=[[0, 4 * P]], base=0, channel_multiplier=1).then_inc(iota_done, 1)
                with pool.Fori(0, HG_HEADS) as hd:
                    for r in range(R):
                        pool.wait_ge(scanned, hd * 2 + min(r + 1, 2))
                        wait_slot(pool, hd, r)
                        for to, a, b in exponents(r)[:3]:
                            last = nc.gpsimd.tensor_tensor(to, a, b, ALU.subtract)
                        last.then_inc(pool_d, 1)

            @block.tensor
            def _(pe):
                pe.wait_ge(v_in, 16)
                with pe.Fori(0, HG_HEADS) as hd:
                    pe.wait_ge(raw_in, 48 * hd + 48)
                    pe.wait_ge(ki_copied, hd * 2 * NG)
                    for n, (x, a, count) in enumerate(in_groups):
                        if 2 <= n < 2 + NG:
                            pe.wait_ge(q_read, hd * NG + n - 1)
                        elif n >= 2:
                            pe.wait_ge(z_read, hd * 2 * NG + n - 1 - NG)
                        for c in range(count):
                            last = nc.tensor.transpose(tp[n % 2][:, c * P:(c + 1) * P], raw[:, x, a + c, :], ident[:])
                        last.then_inc(in_turned, 1)
                    pe.wait_ge(z_read, (hd + 1) * 2 * NG)

                    def turn_keys(n):
                        d, a, count = ki_groups[n]
                        pe.wait_ge(w_ready, hd * R + d + 1)
                        if n >= 2:
                            pe.wait_ge(ki_copied, hd * 2 * NG + n - 1)
                        for c in range(count):
                            last = nc.tensor.transpose(tp[n % 2][:, c * P:(c + 1) * P],
                                                       W[:, d, 1, (a + c) * P:(a + c + 1) * P], ident[:])
                        last.then_inc(ki_turned, 1)

                    def pairs(n):
                        for g, (a, count) in enumerate(CHUNK_GROUPS):
                            if n >= 1:
                                pe.wait_ge(a_done, (hd * NL + n - 1) * NG + g + 1)
                            for c in range(count):
                                cols = slice((a + c) * P, (a + c + 1) * P)
                                slot = (n + 1) % 2
                                lhsT, rhs = (ksum[:, cols], qT[:, cols]) if n == 0 else \
                                    (W[:, slot, 1, cols], W[:, slot, 0, cols])
                                last = nc.tensor.matmul(l_ps[g][:, c * P:(c + 1) * P], lhsT, rhs,
                                                        start=True, stop=True)
                            last.then_inc(l_mm, 1)

                    for n in range(NG):
                        turn_keys(n)
                    pairs(0)
                    for n in range(NG, 2 * NG):
                        turn_keys(n)
                    pe.wait_ge(o_copied, hd * NG)
                    for n, (d, a, count) in enumerate(ki_groups):
                        pe.wait_ge(ki_copied, hd * 2 * NG + n + 1)
                        if n >= 2:
                            pe.wait_ge(s_made, hd * NS + made[n - 2])
                        for c in range(count):
                            last = nc.tensor.matmul(sp_ps[n % 2][:, c * P:(c + 1) * P], kiT[:, d, a + c, :],
                                                    v[:, a + c, bass.ds(hd * P, P)], start=True, stop=True)
                        last.then_inc(ds_mm, 1)
                    for n in range(1, NL):
                        pe.wait_ge(w_ready, hd * R + n + 2)
                        pairs(n)
                    pe.wait_ge(a_done, (hd + 1) * NL * NG)
                    pe.wait_ge(s_made, (hd + 1) * NS)
                    for g, (a, count) in enumerate(CHUNK_GROUPS):
                        if g >= 2:
                            pe.wait_ge(o_copied, hd * NG + g - 1)
                        for c in range(a, a + count):
                            to = sp_ps[g % 2][:, (c - a) * P:(c - a + 1) * P]
                            cols = slice(c * P, (c + 1) * P)
                            dirs = [d for d in range(2) if c not in (starts, ends)[d]]
                            last = nc.tensor.matmul(to, A[:, cols], v[:, c, bass.ds(hd * P, P)],
                                                    start=True, stop=not dirs)
                            for d in dirs:
                                last = nc.tensor.matmul(to, qi[:, d, cols], S[:, d, c, :], start=False,
                                                        stop=(d == dirs[-1]))
                        last.then_inc(o_mm, 1)

            @block.scalar
            def _(act):
                act.wait_ge(chain, 1)
                nc.scalar.activation(lb_e[:], lb_e[:], ACT.Exp).then_inc(lb_ready, 1)
                with act.Fori(0, HG_HEADS) as hd:
                    for n, (x, a, count) in enumerate(in_groups):
                        act.wait_ge(in_turned, hd * 3 * NG + n + 1)
                        src, cols = tp[n % 2][:, 0:count * P], slice(a * P, (a + count) * P)
                        if x == 0:
                            nc.scalar.activation(sgq[:, cols], src, ACT.Sigmoid).then_inc(sg_done, 1)
                        else:
                            nc.scalar.activation(f[:, x - 1, cols], src, ACT.Sigmoid)
                            nc.scalar.activation(k[:, x - 1, cols], src, ACT.Sigmoid, scale=-1.0)\
                              .then_inc(z_read, 1)
                    for d in range(2):
                        act.wait_ge(clamped, hd * 2 + d + 1)
                        nc.scalar.activation(lf[:, d], lf[:, d], ACT.Ln)
                        nc.scalar.activation(f[:, d], f[:, d], ACT.Ln, scale=1.0 / LN_SPLIT).then_inc(ln_done, 1)
                    act.wait_ge(scanned, hd * 2 + 2)
                    nc.scalar.activation(decay[:], E[:, :, :, P], ACT.Exp).then_inc(dec_done, 1)

                    def copy_keys(d):
                        for n in range(d * NG, (d + 1) * NG):
                            _, a, count = ki_groups[n]
                            act.wait_ge(ki_turned, hd * 2 * NG + n + 1)
                            nc.scalar.activation(kiT[:, d, a:a + count, :],
                                                 tp[n % 2][:, 0:count * P].rearrange("p (c t) -> p c t", t=P),
                                                 ACT.Copy).then_inc(ki_copied, 1)

                    for r in range(R):
                        act.wait_ge(pool_d, hd * R + r + 1)
                        z, y = (chunked(W[:, r % 2, x, :]) for x in range(2))
                        if r == 0:
                            nc.scalar.activation(z, e_with[:, 0], ACT.Exp)
                            nc.scalar.activation(y, y, ACT.Exp).then_inc(exp_done, 1)
                        elif r == 1:
                            nc.scalar.activation(y, e_to[:, 1], ACT.Exp)
                            nc.scalar.activation(z, z, ACT.Exp).then_inc(exp_done, 1)
                        else:
                            act.wait_ge(dve_d, hd * LEVELS + r - 1)
                            nc.scalar.activation(W[:, r % 2], W[:, r % 2], ACT.Exp).then_inc(exp_done, 1)
                        if r in (1, 2):
                            copy_keys(r - 1)
                    act.wait_ge(stored, 16 * hd)
                    for g, (a, count) in enumerate(CHUNK_GROUPS):
                        act.wait_ge(o_mm, hd * NG + g + 1)
                        nc.scalar.activation(out[:, a:a + count, :],
                                             sp_ps[g % 2][:, 0:count * P].rearrange("p (c t) -> p c t", t=P),
                                             ACT.Copy).then_inc(o_copied, 1)

            @block.vector
            def _(dve):
                SETUP = 6 + 3 * LEVELS
                step = Steps(SETUP)
                step.round(0)
                dve.wait_ge(lb_in, 32)
                nc.vector.tensor_tensor(lb_e[:], lb[:], lb[:], ALU.subtract).then_inc(chain, 1)
                step.next()
                dve.wait_ge(lb_ready, 1)
                nc.vector.reciprocal(lb_r[:], lb_e[:]).then_inc(chain, 1)
                dve.wait_ge(chain, step.next())
                nc.vector.tensor_tensor(lb_r[:], lb_e[:], lb_r[:], ALU.mult).then_inc(chain, 1)
                dve.wait_ge(chain, step.next())
                nc.vector.tensor_tensor(lb[:], lb_r[:], lb_r[:], ALU.subtract).then_inc(chain, 1)
                dve.wait_ge(chain, step.next())
                nc.vector.tensor_scalar(omlb[:], lb[:], -1.0, 1.0, ALU.mult, ALU.add).then_inc(chain, 1)
                step.next()
                dve.wait_ge(iota_done, 2)
                nc.vector.tensor_tensor(xor_i[:], cols_i[:], rows_i[:], ALU.bitwise_xor).then_inc(chain, 1)
                dve.wait_ge(chain, step.next())
                for n in range(LEVELS):
                    m = P >> (n + 1)
                    nc.vector.tensor_scalar(below[:], xor_i[:], 2.0 * m, None, ALU.is_lt).then_inc(chain, 1)
                    dve.wait_ge(chain, step.next())
                    nc.vector.scalar_tensor_tensor(mask[:, n, :], xor_i[:], float(m), below[:], ALU.is_ge, ALU.mult)\
                      .then_inc(chain, 1)
                    dve.wait_ge(chain, step.next())
                    if n < 4:
                        nc.vector.tensor_copy(diag[:, n, :], ident[:]).then_inc(chain, 1)
                    elif n < 6:
                        nc.vector.memset(E[:, n - 4, :, 0:1], 0.0).then_inc(chain, 1)
                    else:
                        nc.vector.memset(below[:, 0:1], 0.0).then_inc(chain, 1)
                    step.next()
                dve.wait_ge(chain, SETUP)
                PER = 3 * 2
                with dve.Fori(0, HG_HEADS) as hd:
                    count_of = Steps(PER)
                    count_of.base = SETUP + hd * PER
                    dve.wait_ge(o_copied, hd * NG)
                    for n, (a, count) in enumerate(CHUNK_GROUPS):
                        dve.wait_ge(sg_done, hd * NG + n + 1)
                        cols = slice(a * P, (a + count) * P)
                        nc.vector.tensor_tensor(qT[:, cols], tp[n % 2][:, 0:count * P], sgq[:, cols], ALU.mult)\
                          .then_inc(q_read, 1)
                    for d in range(2):
                        dve.wait_ge(z_read, hd * 2 * NG + NG * (d + 1))
                        one_less, low = omlb[:, d, bass.ds(hd, 1)], lb[:, d, bass.ds(hd, 1)]
                        nc.vector.tensor_scalar(k[:, d], k[:, d], one_less, None, ALU.mult).then_inc(chain, 1)
                        count_of.next()
                        nc.vector.tensor_scalar(f[:, d], f[:, d], one_less, low, ALU.mult, ALU.add).then_inc(chain, 1)
                        dve.wait_ge(chain, count_of.next())
                        nc.vector.tensor_scalar(lf[:, d], f[:, d], LN_SPLIT, None, ALU.max).then_inc(chain, 1)
                        dve.wait_ge(chain, count_of.next())
                        nc.vector.tensor_scalar(f[:, d], f[:, d], F_MIN, LN_SPLIT, ALU.max, ALU.min)\
                          .then_inc(clamped, 1)
                    nc.vector.tensor_tensor(ksum[:], k[:, 0], k[:, 1], ALU.add)
                    for d in range(2):
                        dve.wait_ge(ln_done, hd * 2 + d + 1)
                        for c in range(NT):
                            last = nc.vector.tensor_tensor_scan(E[:, d, c, 1:P + 1], lf[:, d, c * P:(c + 1) * P],
                                                                f[:, d, c * P:(c + 1) * P], 0.0, ALU.add, ALU.add)
                        last.then_inc(scanned, 1)

                    def differences(r):
                        if r >= 2:
                            wait_slot(dve, hd, r)
                            to, a, b = exponents(r)[3]
                            nc.vector.tensor_tensor(to, a, b, ALU.subtract).then_inc(dve_d, 1)

                    def weights(r):
                        dve.wait_ge(exp_done, hd * R + r + 1)
                        z, y = W[:, r % 2, 0], W[:, r % 2, 1]
                        nc.vector.tensor_tensor(qi[:, r] if r < 2 else z, z, qT[:], ALU.mult)
                        if r < 2:
                            nc.vector.tensor_tensor(y, y, k[:, r], ALU.mult).then_inc(w_ready, 1)
                            return
                        m = P >> (r - 1)
                        for side in range(2):
                            part = halves(chunked(y), m, side)
                            last = nc.vector.tensor_tensor(part, part, halves(chunked(k[:, side]), m, side), ALU.mult)
                        last.then_inc(w_ready, 1)

                    def gather(n):
                        for g, (a, count) in enumerate(CHUNK_GROUPS):
                            cols, width = slice(a * P, (a + count) * P), count * P
                            if n == 0:
                                dve.wait_ge(l_mm, (hd * NL + n) * NG + g + 1)
                                nc.vector.tensor_tensor(A[:, cols], l_ps[g][:, 0:width],
                                                        diag[:, 0:count].rearrange("p c t -> p (c t)"), ALU.mult)\
                                  .then_inc(a_done, 1)
                            else:
                                products = held(dve, (hd * NL + n) * NG + g + 1)
                                before = held(dve, (hd * NL + n - 1) * NG + g + 1)
                                dve.wait_ge(chain, SETUP)
                                dve.wait_ge(l_mm, products)
                                dve.wait_ge(a_done, before)
                                nc.vector.copy_predicated(A[:, cols], mask[:, n - 1, 0:width], l_ps[g][:, 0:width])\
                                  .then_inc(a_done, 1)

                    def states():
                        dve.wait_ge(dec_done, hd + 1)
                        steps = 0
                        for n, (d, a, count) in enumerate(ki_groups):
                            dve.wait_ge(ds_mm, hd * 2 * NG + n + 1)
                            order = list(range(a, a + count))
                            for c in order if d == 0 else reversed(order):
                                to = c + 1 - 2 * d
                                if c in (ends, starts)[d]:
                                    continue
                                steps += 1
                                add = sp_ps[n % 2][:, (c - a) * P:(c - a + 1) * P]
                                if c in (starts, ends)[d]:
                                    nc.vector.tensor_copy(S[:, d, to, :], add).then_inc(s_made, 1)
                                else:
                                    nc.vector.scalar_tensor_tensor(S[:, d, to, :], S[:, d, c, :], decay[:, d, c:c + 1],
                                                                   add, ALU.mult, ALU.add).then_inc(s_made, 1)
                                dve.wait_ge(s_made, hd * NS + steps)

                    weights(0)
                    weights(1)
                    differences(2)
                    gather(0)
                    for r in range(2, R):
                        if r + 1 < R:
                            differences(r + 1)
                        weights(r)
                        if r == 2:
                            states()
                        if r >= 3:
                            gather(r - 2)
                    gather(R - 2)


def stage_mix(nc, ident, h, aT, o, norm_g, w_na, w_hg, mix):
    KB = NAW // P
    with ExitStack() as ctx:
        s = Stage(nc, ctx, "mix")
        wraw = s.sb("wraw", [P, KB, D])
        w_hi, w_lo = s.sb("w_hi", [P, 2, KB, D], F32R), s.sb("w_lo", [P, 2, KB, D], F32R)
        a_in, o_in, g_in = s.sb("a_in", [P, 2, KB, P]), s.sb("o_in", [P, 2, HGW]), s.sb("g_in", [P, 2, HGW])
        gates = s.sb("gates", [P, 2, 2, D])
        norm_all = s.sb("norm_all", [P, HGW])
        act_hi, act_lo = (s.sb(n, [P, 2, 2, KB, P], F32R) for n in ("act_hi", "act_lo"))
        sg, gg, sq, on, oh = (s.sb(n, [P, 2, HGW]) for n in ("sg", "gg", "sq", "on", "oh"))
        ss, rstd, mhalf = s.sb("ss", [P, 2, HG_HEADS]), s.sb("rstd", [P, 2, HG_HEADS]), s.sb("mhalf", [P, HG_HEADS])
        prod = s.sb("prod", [P, 2, 2, 2, 512])
        out = s.sb("out", [P, 2, D])
        tp = [s.ps(f"tp{u}", [P, 512]) for u in range(2)]
        acc = [[s.ps(f"acc{x}{b}", [P, 512]) for b in range(2)] for x in range(2)]
        w_in, w_hi_done, w_lo_done, norm_in = (s.sem(n) for n in ("w_in", "w_hi_done", "w_lo_done", "norm_in"))
        loaded, gates_in, stored = s.sems("loaded", 2), s.sems("gates_in", 2), s.sems("stored", 2)
        multiplied = s.sems("multiplied", 2)
        formed, used, gates_done = s.sems("formed", 2), s.sems("used", 2), s.sem("gates_done")
        (sg_done, a_hi, a_lo, gg_half, gg_done, half_made, squared, scaled, ss_done, var_done, rstd_done, oh_done,
         oh_turned, o_hi, acc_done, prod_done) = (s.sem(n) for n in (
             "sg_done", "a_hi", "a_lo", "gg_half", "gg_done", "half_made", "squared", "scaled", "ss_done",
             "var_done", "rstd_done", "oh_done", "oh_turned", "o_hi", "acc_done", "prod_done"))
        out_done = s.sems("out_done", 2)
        with nc.Block() as block:
            @block.sync
            def _(sp):
                for b, w in enumerate((w_na, w_hg)):
                    sp.wait_ge(w_lo_done, b)
                    sp.dma_start(wraw[:], w.rearrange("(k p) n -> p k n", p=P)).then_inc(w_in, 16)
                    if b == 0:
                        sp.dma_start(norm_all[:], rows_of(norm_g, HGW)).then_inc(norm_in, 16)

                def load(t, u, r):
                    rows = bass.ds(t * P, P)
                    sp.wait_ge(formed[u], r)
                    sp.dma_start(a_in[:, u], aT[:, rows].rearrange("(k p) t -> p k t", p=P)).then_inc(loaded[u], 16)
                    sp.dma_start(o_in[:, u], o[rows, :]).then_inc(loaded[u], 16)
                    sp.dma_start(g_in[:, u], h[rows, COL_G:COL_G + HGW]).then_inc(loaded[u], 16)

                def load_gates(t, u, r):
                    sp.wait_ge(used[u], r)
                    sp.dma_start(gates[:, u].rearrange("p b n -> p (b n)"),
                                 h[bass.ds(t * P, P), COL_GATE:COL_GATE + 2 * D]).then_inc(gates_in[u], 16)

                in_steps(sp, [(0, load), (1, load_gates)])

            @block.scalar
            def _(act):
                for b in range(2):
                    act.wait_ge(w_in, 16 * b + 16)
                    nc.scalar.activation(w_hi[:, b], wraw[:], ACT.Copy).then_inc(w_hi_done, 1)

                def prepare(t, u, r):
                    act.wait_ge(loaded[u], 48 * r + 48)
                    act.wait_ge(formed[u], r)
                    nc.scalar.activation(sg[:, u], g_in[:, u], ACT.Sigmoid).then_inc(sg_done, 1)

                def form(t, u, r):
                    act.wait_ge(multiplied[u], r)
                    nc.scalar.activation(act_hi[:, u, 0], a_in[:, u], ACT.Copy).then_inc(a_hi, 1)
                    act.wait_ge(oh_turned, t + 1)
                    nc.scalar.activation(act_hi[:, u, 1], tp[u][:].rearrange("p (k c) -> p k c", k=KB), ACT.Copy)\
                      .then_inc(o_hi, 1)

                def open_gates(t, u, r):
                    act.wait_ge(gates_in[u], 16 * r + 16)
                    nc.scalar.activation(gates[:, u], gates[:, u], ACT.Sigmoid).then_inc(gates_done, 1)

                in_steps(act, [(0, prepare), (1, form), (2, open_gates)])

            @block.gpsimd
            def _(pool):
                nc.gpsimd.memset(mhalf[:], -0.5).then_inc(half_made, 1)
                pool.wait_ge(norm_in, 16)
                pool.wait_ge(half_made, 1)

                def prepare(t, u, r):
                    pool.wait_ge(sg_done, t + 1)
                    nc.gpsimd.tensor_tensor(gg[:, u], g_in[:, u], sg[:, u], ALU.mult).then_inc(gg_half, 1)
                    pool.wait_ge(gg_half, t + 1)
                    nc.gpsimd.tensor_tensor(gg[:, u], gg[:, u], norm_all[:], ALU.mult).then_inc(gg_done, 1)
                    count = held(pool, t + 1)
                    pool.wait_ge(half_made, 1)
                    pool.wait_ge(ss_done, count)
                    nc.gpsimd.tensor_scalar(ss[:, u], ss[:, u], 1.0 / P, RMS_EPS, ALU.mult, ALU.add)\
                      .then_inc(var_done, 1)
                    pool.wait_ge(var_done, t + 1)
                    nc.gpsimd.tensor_tensor(rstd[:, u], ss[:, u], mhalf[:], ALU.pow).then_inc(rstd_done, 1)

                def add(t, u, r):
                    pool.wait_ge(stored[u], 16 * r)
                    for x in range(2):
                        if x == 0:
                            pool.wait_ge(prod_done, t + 1)
                        else:
                            pool.wait_ge(used[u], r + 1)
                        last = nc.gpsimd.tensor_tensor(out[:, u, x * 512:(x + 1) * 512], prod[:, u, x, 0],
                                                       prod[:, u, x, 1], ALU.add)
                    last.then_inc(out_done[u], 1)
                    count = held(pool, r + 1)
                    pool.wait_ge(half_made, 1)
                    pool.wait_ge(out_done[u], count)
                    pool.dma_start(mix[bass.ds(t * P, P), :], out[:, u]).then_inc(stored[u], 16)

                in_steps(pool, [(0, prepare), (3, add)])
                for u in range(2):
                    pool.wait_ge(stored[u], 16 * (NT // 2))

            @block.vector
            def _(dve):
                for b in range(2):
                    dve.wait_ge(w_hi_done, b + 1)
                    nc.vector.tensor_tensor(w_lo[:, b], wraw[:], w_hi[:, b].bitcast(F32), ALU.subtract)\
                      .then_inc(w_lo_done, 1)

                def prepare(t, u, r):
                    dve.wait_ge(loaded[u], 48 * r + 48)
                    nc.vector.tensor_tensor(sq[:, u], o_in[:, u], o_in[:, u], ALU.mult).then_inc(squared, 1)
                    dve.wait_ge(squared, t + 1)
                    nc.vector.tensor_reduce(ss[:, u], sq[:, u].rearrange("p (h c) -> p h c", c=P), AX.X, ALU.add)\
                      .then_inc(ss_done, 1)

                def form(t, u, r):
                    dve.wait_ge(a_hi, t + 1)
                    nc.vector.tensor_tensor(act_lo[:, u, 0], a_in[:, u], act_hi[:, u, 0].bitcast(F32), ALU.subtract)\
                      .then_inc(a_lo, 1)
                    dve.wait_ge(rstd_done, t + 1)
                    nc.vector.tensor_tensor(on[:, u].rearrange("p (h c) -> p h c", c=P),
                                            o_in[:, u].rearrange("p (h c) -> p h c", c=P),
                                            rstd[:, u].unsqueeze(2).to_broadcast([P, HG_HEADS, P]), ALU.mult)\
                      .then_inc(scaled, 1)
                    dve.wait_ge(scaled, t + 1)
                    dve.wait_ge(gg_done, t + 1)
                    nc.vector.tensor_tensor(oh[:, u], on[:, u], gg[:, u], ALU.mult).then_inc(oh_done, 1)

                def split(t, u, r):
                    dve.wait_ge(o_hi, t + 1)
                    nc.vector.tensor_tensor(act_lo[:, u, 1], tp[u][:].rearrange("p (k c) -> p k c", k=KB),
                                            act_hi[:, u, 1].bitcast(F32), ALU.subtract)\
                      .then_inc(formed[u], 1)

                def weigh(t, u, r):
                    dve.wait_ge(gates_done, t + 1)
                    dve.wait_ge(out_done[u], r)
                    for x in range(2):
                        if x == 0:
                            dve.wait_ge(acc_done, t + 1)
                        else:
                            dve.wait_ge(multiplied[u], r + 1)
                        for b in range(2):
                            last = nc.vector.tensor_tensor(prod[:, u, x, b], acc[x][b][:],
                                                           gates[:, u, b, x * 512:(x + 1) * 512], ALU.mult)
                        last.then_inc(prod_done if x == 0 else used[u], 1)

                in_steps(dve, [(0, prepare), (1, form), (3, weigh), (1, split)])

            @block.tensor
            def _(pe):
                pe.wait_ge(w_lo_done, 2)

                def turn(t, u, r):
                    pe.wait_ge(oh_done, t + 1)
                    for k in range(KB):
                        last = nc.tensor.transpose(tp[u][:, k * P:(k + 1) * P], oh[:, u, k * P:(k + 1) * P], ident[:])
                    last.then_inc(oh_turned, 1)

                def product(t, u, r):
                    pe.wait_ge(a_lo, t + 1)
                    pe.wait_ge(formed[u], r + 1)
                    for x in range(2):
                        cols = slice(x * 512, (x + 1) * 512)
                        if x == 0:
                            pe.wait_ge(prod_done, t)
                        else:
                            pe.wait_ge(used[1 - u], r + u)
                        for b in range(2):
                            for k in range(KB):
                                hi, lo = act_hi[:, u, b, k, :], act_lo[:, u, b, k, :]
                                nc.tensor.matmul(acc[x][b][:], hi, w_hi[:, b, k, cols], start=(k == 0), stop=False)
                                nc.tensor.matmul(acc[x][b][:], hi, w_lo[:, b, k, cols], start=False, stop=False)
                                last = nc.tensor.matmul(acc[x][b][:], lo, w_hi[:, b, k, cols], start=False,
                                                        stop=(k == KB - 1))
                        last.then_inc(acc_done if x == 0 else multiplied[u], 1)

                in_steps(pe, [(1, turn), (2, product)])


def stage_out(nc, ident, mix, xln, w_out, g, b, w_router, x1, y, affT):
    with ExitStack() as ctx:
        s = Stage(nc, ctx, "out")
        wraw = s.sb("wraw", [P, 4, D])
        w_hi, w_lo = s.sb("w_hi", [P, KD, D], F32R), s.sb("w_lo", [P, KD, D], F32R)
        wr = s.sb("wr", [P, KD, NE])
        g_all, b_all = s.sb("g_all", [P, D]), s.sb("b_all", [P, D])
        mix_in, x_in = s.sb("mix_in", [P, 2, D]), s.sb("x_in", [P, 2, D])
        m_hi, m_lo = s.sb("m_hi", [P, 2, KD, P], F32R), s.sb("m_lo", [P, 2, KD, P], F32R)
        x1_sb, y_sb = s.sb("x1_sb", [P, 2, D]), s.sb("y_sb", [P, 2, D])
        x1T = s.sb("x1T", [P, KD, P])
        stats, mv, veps, rstd, mhalf = (s.sb(n, sh) for n, sh in (
            ("stats", [P, 2, 6]), ("mv", [P, 2]), ("veps", [P, 1]), ("rstd", [P, 1]), ("mhalf", [P, 1])))
        nmax, total, inv, aff = (s.sb(n, sh) for n, sh in (
            ("nmax", [P, 1]), ("total", [P, 1]), ("inv", [P, 1]), ("aff", [P, NE])))
        tp, tx = s.ps("tp", [P, D]), s.ps("tx", [P, D])
        acc = [s.ps(f"acc{x}", [P, 512]) for x in range(2)]
        lg, at = s.ps("lg", [P, NE]), s.ps("at", [NE, P])
        w_in, w_hi_done, w_lo_done, small_in = (s.sem(n) for n in ("w_in", "w_hi_done", "w_lo_done", "small_in"))
        x_read, x_loaded, m_turned, x1_turned = (s.sems(n, 2) for n in ("x_read", "x_loaded", "m_turned", "x1_turned"))
        summed = s.sems("summed", 2)
        loaded, stored_x, stored_y = s.sems("loaded", 2), s.sems("stored_x", 2), s.sems("stored_y", 2)
        (m_hi_done, m_lo_done, acc_done, chain, var_ready, var_eps, rstd_ready, centred, x1_done,
         y_done, x1_copied, lg_done, maxed, exp_done, inverted, aff_done, aff_turned, aff_copied,
         half_made) = (s.sem(n) for n in (
             "m_hi_done", "m_lo_done", "acc_done", "chain", "var_ready", "var_eps",
             "rstd_ready", "centred", "x1_done", "y_done", "x1_copied", "lg_done", "maxed", "exp_done",
             "inverted", "aff_done", "aff_turned", "aff_copied", "half_made"))
        w_view = w_out.rearrange("(k p) n -> p k n", p=P)
        with nc.Block() as block:
            @block.sync
            def _(sp):
                for v in range(2):
                    sp.wait_ge(w_lo_done, v)
                    sp.dma_start(wraw[:], w_view[:, 4 * v:4 * v + 4, :]).then_inc(w_in, 16)
                    if v == 0:
                        sp.dma_start(wr[:], w_router.rearrange("(k p) e -> p k e", p=P)).then_inc(small_in, 16)
                        sp.dma_start(g_all[:], rows_of(g, D)).then_inc(small_in, 16)
                        sp.dma_start(b_all[:], rows_of(b, D)).then_inc(small_in, 16)

                def load(t, u, r):
                    sp.wait_ge(m_turned[u], r)
                    sp.dma_start(mix_in[:, u], mix[bass.ds(t * P, P), :]).then_inc(loaded[u], 16)

                def load_x(t, u, r):
                    sp.wait_ge(x_read[u], r)
                    sp.dma_start(x_in[:, u], xln[bass.ds(t * P, P), :]).then_inc(x_loaded[u], 16)

                in_steps(sp, [(0, load), (1, load_x)])

            @block.scalar
            def _(act):
                for v in range(2):
                    act.wait_ge(w_in, 16 * v + 16)
                    nc.scalar.activation(w_hi[:, 4 * v:4 * v + 4], wraw[:], ACT.Copy).then_inc(w_hi_done, 1)

                def split(t, u, r):
                    act.wait_ge(m_turned[u], r + 1)
                    for x in range(2):
                        last = nc.scalar.activation(m_hi[:, u, 4 * x:4 * x + 4],
                                                    tp[:, x * 512:(x + 1) * 512].rearrange("p (k c) -> p k c", k=4),
                                                    ACT.Copy)
                    last.then_inc(m_hi_done, 1)

                def scale(t, u, r):
                    act.wait_ge(x1_done, t + 1)
                    act.wait_ge(stored_y[u], 16 * r)
                    nc.scalar.activation(y_sb[:, u], x1_sb[:, u], ACT.Copy, scale=ALPHA).then_inc(y_done, 1)

                def copy_x1(t, u, r):
                    act.wait_ge(x1_turned[u], r + 1)
                    act.wait_ge(lg_done, t)
                    for x in range(2):
                        last = nc.scalar.activation(x1T[:, 4 * x:4 * x + 4],
                                                    tx[:, x * 512:(x + 1) * 512].rearrange("p (k c) -> p k c", k=4),
                                                    ACT.Copy)
                    last.then_inc(x1_copied, 1)

                def exp(t, u, r):
                    act.wait_ge(maxed, t + 1)
                    act.wait_ge(aff_turned, t)
                    nc.scalar.activation(aff[:], lg[:], ACT.Exp, bias=nmax[:], accum_out=total[:]).then_inc(exp_done, 1)

                in_steps(act, [(0, split), (3, copy_x1), (2, scale), (4, exp)])

            @block.gpsimd
            def _(pool):
                nc.gpsimd.memset(mhalf[:], -0.5).then_inc(half_made, 1)
                pool.wait_ge(half_made, 1)

                def norm(t, u, r):
                    count = held(pool, t + 1)
                    pool.wait_ge(half_made, 1)
                    pool.wait_ge(var_ready, count)
                    nc.gpsimd.tensor_scalar(veps[:], mv[:, 1:2], LN_EPS, None, ALU.add).then_inc(var_eps, 1)
                    pool.wait_ge(var_eps, t + 1)
                    nc.gpsimd.tensor_tensor(rstd[:], veps[:], mhalf[:], ALU.pow).then_inc(rstd_ready, 1)
                    rows = bass.ds(t * P, P)
                    pool.wait_ge(x1_done, t + 1)
                    pool.dma_start(x1[rows, :], x1_sb[:, u]).then_inc(stored_x[u], 16)
                    count = held(pool, t + 1)
                    pool.wait_ge(half_made, 1)
                    pool.wait_ge(y_done, count)
                    pool.dma_start(y[rows, :], y_sb[:, u]).then_inc(stored_y[u], 16)

                in_steps(pool, [(2, norm)])
                for u in range(2):
                    pool.wait_ge(stored_x[u], 16 * (NT // 2))
                    pool.wait_ge(stored_y[u], 16 * (NT // 2))

            @block.vector
            def _(dve):
                for v in range(2):
                    dve.wait_ge(w_hi_done, v + 1)
                    nc.vector.tensor_tensor(w_lo[:, 4 * v:4 * v + 4], wraw[:],
                                            w_hi[:, 4 * v:4 * v + 4].bitcast(F32), ALU.subtract)\
                      .then_inc(w_lo_done, 1)
                dve.wait_ge(small_in, 48)

                def split(t, u, r):
                    dve.wait_ge(m_hi_done, t + 1)
                    for x in range(2):
                        last = nc.vector.tensor_tensor(m_lo[:, u, 4 * x:4 * x + 4],
                                                       tp[:, x * 512:(x + 1) * 512].rearrange("p (k c) -> p k c", k=4),
                                                       m_hi[:, u, 4 * x:4 * x + 4].bitcast(F32), ALU.subtract)
                    last.then_inc(m_lo_done, 1)

                def add_up(t, u, r):
                    dve.wait_ge(x_loaded[u], 16 * r + 16)
                    for x in range(2):
                        cols = slice(x * 512, (x + 1) * 512)
                        dve.wait_ge(acc_done, 2 * t + x + 1)
                        nc.vector.scalar_tensor_tensor(x_in[:, u, cols], x_in[:, u, cols], ALPHA, acc[x][:],
                                                       ALU.mult, ALU.add).then_inc(summed[x], 1)
                    for x in range(2):
                        dve.wait_ge(summed[x], t + 1)
                        nc.vector.bn_stats(stats[:, x, :], x_in[:, u, x * 512:(x + 1) * 512]).then_inc(chain, 1)
                    count = held(dve, 3 * t + 2)
                    dve.wait_ge(small_in, 48)
                    dve.wait_ge(chain, count)
                    nc.vector.bn_aggr(mv[:], stats[:]).then_inc(var_ready, 1)

                def centre(t, u, r):
                    dve.wait_ge(stored_x[u], 16 * r)
                    dve.wait_ge(stored_y[u], 16 * r)
                    dve.wait_ge(x1_turned[u], r)
                    dve.wait_ge(var_ready, t + 1)
                    dve.wait_ge(rstd_ready, t + 1)
                    nc.vector.tensor_scalar(x1_sb[:, u], x_in[:, u], mv[:, 0:1], rstd[:], ALU.subtract, ALU.mult)\
                      .then_inc(x_read[u], 1)
                    dve.wait_ge(x_read[u], r + 1)
                    nc.vector.tensor_tensor(x1_sb[:, u], x1_sb[:, u], g_all[:], ALU.mult).then_inc(chain, 1)
                    dve.wait_ge(chain, 3 * t + 3)
                    nc.vector.tensor_tensor(x1_sb[:, u], x1_sb[:, u], b_all[:], ALU.add).then_inc(x1_done, 1)

                def find_max(t, u, r):
                    dve.wait_ge(lg_done, t + 1)
                    nc.vector.tensor_reduce(nmax[:], lg[:], AX.X, ALU.max, negate=True).then_inc(maxed, 1)

                def normalise(t, u, r):
                    dve.wait_ge(exp_done, t + 1)
                    nc.vector.reciprocal(inv[:], total[:]).then_inc(inverted, 1)
                    dve.wait_ge(inverted, t + 1)
                    nc.vector.tensor_scalar(aff[:], aff[:], inv[:], None, ALU.mult).then_inc(aff_done, 1)

                def keep(t, u, r):
                    dve.wait_ge(aff_turned, t + 1)
                    nc.vector.tensor_copy(affT[:, bass.ds(t * P, P)], at[:]).then_inc(aff_copied, 1)

                in_steps(dve, [(4, find_max), (2, add_up), (0, split), (2, centre), (4, normalise), (5, keep)])

            @block.tensor
            def _(pe):
                pe.wait_ge(w_lo_done, 2)

                def turn(t, u, r):
                    pe.wait_ge(loaded[u], 16 * r + 16)
                    pe.wait_ge(m_lo_done, t)
                    for k in range(KD):
                        last = nc.tensor.transpose(tp[:, k * P:(k + 1) * P], mix_in[:, u, k * P:(k + 1) * P], ident[:])
                    last.then_inc(m_turned[u], 1)

                def product(t, u, r):
                    pe.wait_ge(m_lo_done, t + 1)
                    for x in range(2):
                        cols = slice(x * 512, (x + 1) * 512)
                        pe.wait_ge(summed[x], t)
                        for k in range(KD):
                            hi, lo = m_hi[:, u, k, :], m_lo[:, u, k, :]
                            nc.tensor.matmul(acc[x][:], hi, w_hi[:, k, cols], start=(k == 0), stop=False)
                            nc.tensor.matmul(acc[x][:], hi, w_lo[:, k, cols], start=False, stop=False)
                            last = nc.tensor.matmul(acc[x][:], lo, w_hi[:, k, cols], start=False, stop=(k == KD - 1))
                        last.then_inc(acc_done, 1)

                def turn_x1(t, u, r):
                    pe.wait_ge(x1_done, t + 1)
                    pe.wait_ge(x1_copied, t)
                    for k in range(KD):
                        last = nc.tensor.transpose(tx[:, k * P:(k + 1) * P], x1_sb[:, u, k * P:(k + 1) * P], ident[:])
                    last.then_inc(x1_turned[u], 1)

                def logits(t, u, r):
                    pe.wait_ge(x1_copied, t + 1)
                    pe.wait_ge(exp_done, t)
                    for k in range(KD):
                        last = nc.tensor.matmul(lg[:], x1T[:, k, :], wr[:, k, :], start=(k == 0), stop=(k == KD - 1))
                    last.then_inc(lg_done, 1)

                def turn_aff(t, u, r):
                    pe.wait_ge(aff_done, t + 1)
                    pe.wait_ge(aff_copied, t)
                    nc.tensor.transpose(at[:], aff[:], ident[:]).then_inc(aff_turned, 1)

                in_steps(pe, [(5, turn_aff), (0, turn), (1, product), (2, turn_x1), (3, logits)])


def stage_choose(nc, ident, affT, gates, picks):
    with ExitStack() as ctx:
        s = Stage(nc, ctx, "choose")
        best, at, at_f = s.sb("best", [NE, TOK]), s.sb("at", [NE, TOK], U32), s.sb("at_f", [NE, TOK])
        tp = s.ps("tp", [P, 2, 2, NE])
        cleared, chain, found, turned, made = (s.sem(n) for n in ("cleared", "chain", "found", "turned", "made"))
        first_slot = (0, CAPS[0])
        with nc.Block() as block:
            @block.gpsimd
            def _(pool):
                for n in range(2):
                    nc.gpsimd.memset(picks[n][:], 0).then_inc(cleared, 1)

            @block.vector
            def _(dve):
                steps = 0
                for n, (start, count) in enumerate(SEQS):
                    row = affT[:, start:start + count]
                    for c in range(first_slot[n], first_slot[n] + CAPS[n], 8):
                        for op in range(3):
                            if steps:
                                dve.wait_ge(chain, steps)
                            eight = best[:, c:c + 8]
                            if op == 0:
                                ins = nc.vector.max(eight, row)
                            elif op == 1:
                                ins = nc.vector.max_index(at[:, c:c + 8], eight, row)
                            else:
                                ins = nc.vector.match_replace(out=row, in_to_replace=eight, in_values=row,
                                                              imm_value=-1.0)
                            ins.then_inc(chain, 1)
                            steps += 1
                dve.wait_ge(chain, steps)
                for n, (start, _) in enumerate(SEQS):
                    cols = slice(first_slot[n], first_slot[n] + CAPS[n])
                    nc.vector.tensor_scalar(at_f[:, cols], at[:, cols], float(start), None, ALU.add).then_inc(found, 1)
                dve.wait_ge(turned, 1)
                dve.wait_ge(cleared, 2)
                for n in range(2):
                    nc.vector.tensor_copy(gates[n][:], tp[0:CAPS[n], n, 0, :]).then_inc(made, 1)
                    nc.vector.tensor_copy(picks[n][:, 0:NE], tp[0:CAPS[n], n, 1, :]).then_inc(made, 1)
                dve.wait_ge(made, 4)

            @block.tensor
            def _(pe):
                pe.wait_ge(found, 2)
                for n in range(2):
                    cols = slice(first_slot[n], first_slot[n] + CAPS[n])
                    nc.tensor.transpose(tp[0:CAPS[n], n, 0, :], best[:, cols], ident[0:NE, 0:NE])
                    last = nc.tensor.transpose(tp[0:CAPS[n], n, 1, :], at_f[:, cols], ident[0:NE, 0:NE])
                last.then_inc(turned, 1)


def stage_experts(nc, ident, x1, w_gate, w_up, w_down, gates, picks, y):
    RING, PIECE = 6, KD * 512
    UNITS = NFT // 2
    SLICES = 4
    CP, CS = CAPS
    with ExitStack() as ctx:
        s = Stage(nc, ctx, "moe")
        ring = s.sb("ring", [P, RING, PIECE])
        rows_s, rows_p = s.sb("rows_s", [CS, D]), s.sb("rows_p", [CP, D])
        xT = s.sb("xT", [P, KD, TOK])
        sil, hdn = s.sb("sil", [P, 2, 2, TOK]), s.sb("hdn", [P, NFT, TOK])
        outT = s.sb("outT", [P, KD, TOK])
        out_s, out_p = s.sb("out_s", [CS, D]), s.sb("out_p", [CP, D])
        at_in = [s.sb(f"at_in{n}", [CAPS[n], 1], U32) for n in range(2)]
        at_out = [s.sb(f"at_out{n}", [CAPS[n], 1], U32) for n in range(2)]
        gate_ps = [s.ps(f"gate{b}", [P, 2, TOK]) for b in range(2)]
        up_ps = [s.ps(f"up{b}", [P, 2, TOK]) for b in range(2)]
        down_ps = [s.ps(f"down{b}", [P, 2, TOK]) for b in range(2)]
        turn_ps = [s.ps(f"turn{b}", [P, 512]) for b in range(2)]
        w_ready = s.sems("w_ready", RING)
        gate_mm, up_mm, down_mm = s.sems("gate_mm", 2), s.sems("up_mm", 2), s.sems("down_mm", SLICES)
        silu_done, hdn_made, down_copied = s.sems("silu_done", 2), s.sems("hdn_made", 2), s.sems("down_copied", 2)
        gathered, in_turned, in_read = s.sem("gathered"), s.sem("in_turned"), s.sem("in_read")
        out_turned, out_read, added = s.sem("out_turned"), s.sem("out_read"), s.sem("added")
        at_ready = s.sem("at_ready")

        def fresh_piece(e, n):
            if n in (0, 1):
                return (gate_mm, up_mm)[n][1], SLICES * e
            if n < RING:
                return down_mm[n - 2], e
            return (gate_mm, up_mm)[n % 2][1], SLICES * e + (n - RING) // 2 + 1

        with nc.Block() as block:
            @block.sync
            def _(sp):
                with sp.Fori(0, NE) as e:
                    for n in range(3 * SLICES):
                        sp.wait_ge(*fresh_piece(e, n))
                        to = ring[:, n % RING, :]
                        if n < 2 * SLICES:
                            w, q = (w_gate, w_up)[n % 2], n // 2
                            src = w[bass.ds(e * D, D), q * 512:(q + 1) * 512]
                        else:
                            q = n - 2 * SLICES
                            src = w_down[bass.ds(e * FF, FF), q * 256:(q + 1) * 256]
                        to = to.rearrange("p (k n) -> p k n", n=src.shape[1])
                        sp.dma_start(to, src.rearrange("(k p) n -> p k n", p=P)).then_inc(w_ready[n % RING], 16)

            @block.gpsimd
            def _(pool):
                def gather(e):
                    for n in range(2):
                        nc.gpsimd.tensor_copy(at_in[n][:], picks[n][:, bass.ds(e, 1)]).then_inc(at_ready, 1)
                    count = held(pool, 4 * e + 2)
                    pool.wait_ge(at_ready, 2)
                    pool.wait_ge(at_ready, count)
                    for n, to in enumerate((rows_p, rows_s)):
                        pool.indirect_dma_start(to[:], None, x1, bass.IndirectOffsetOnAxis(at_in[n][:], 0))\
                            .then_inc(gathered, 16)

                gather(0)
                with pool.Fori(0, NE) as e:
                    pool.wait_ge(in_turned, 3 * e + 3)
                    pool.wait_ge(added, 32 * e)
                    for n in range(2):
                        nc.gpsimd.tensor_copy(at_out[n][:], picks[n][:, bass.ds(e, 1)]).then_inc(at_ready, 1)
                    gather(e + 1)
                    count0 = held(pool, 4 * e + 6)
                    count1 = held(pool, 4 * e + 4)
                    pool.wait_ge(gathered, 32)
                    pool.wait_ge(at_ready, count0)
                    pool.wait_ge(out_read, count1)
                    for n, src in enumerate((out_p, out_s)):
                        pool.indirect_dma_start(y, bass.IndirectOffsetOnAxis(at_out[n][:], 0), src[:], None,
                                                compute_op=ALU.add).then_inc(added, 16)
                pool.wait_ge(added, 32 * NE)
                pool.wait_ge(gathered, 32 * (NE + 1))

            @block.tensor
            def _(pe):
                def turn_in(e):
                    pe.wait_ge(gathered, 32 * e + 32)
                    for j in range(3):
                        if j == 2:
                            count = held(pe, 3 * e + 1)
                            pe.wait_ge(gathered, 32)
                            pe.wait_ge(in_read, count)
                            for k in range(KD):
                                last = nc.tensor.transpose(turn_ps[0][:, k * CP:(k + 1) * CP],
                                                           rows_p[:, k * P:(k + 1) * P], ident[0:CP, 0:CP])
                        else:
                            for k in range(4):
                                last = nc.tensor.transpose(turn_ps[j][:, k * P:(k + 1) * P],
                                                           rows_s[:, (4 * j + k) * P:(4 * j + k + 1) * P], ident[:])
                        last.then_inc(in_turned, 1)

                def turn_out(e):
                    for j in range(4):
                        if j < 2:
                            pe.wait_ge(in_read, 3 * e + 5 + j)
                        else:
                            pe.wait_ge(out_read, 4 * e + j - 1)
                        part, b = (slice(0, CS), slice(CS, TOK))[j % 2], 1 - j % 2
                        if j == 0:
                            pe.wait_ge(down_copied[0], 2 * e + 1)
                            pe.wait_ge(down_copied[1], 2 * e + 1)
                        if j == 2:
                            pe.wait_ge(down_copied[0], 2 * e + 2)
                            pe.wait_ge(down_copied[1], 2 * e + 2)
                        for k in range(4):
                            last = nc.tensor.transpose(turn_ps[b][0:part.stop - part.start, k * P:(k + 1) * P],
                                                       outT[:, 4 * (j // 2) + k, part], ident[:])
                        last.then_inc(out_turned, 1)

                turn_in(0)
                with pe.Fori(0, NE) as e:
                    pe.wait_ge(in_read, 3 * e + 3)
                    for n in range(UNITS):
                        q, b = n // 2, n % 2
                        for w, ps, free, done in ((0, gate_ps, silu_done, gate_mm), (1, up_ps, hdn_made, up_mm)):
                            piece = 2 * q + w
                            pe.wait_ge(w_ready[piece % RING], 32 * e + 16 * (piece // RING) + 16)
                            pe.wait_ge(free[b], 4 * e + q)
                            weights = ring[:, piece % RING, :].rearrange("p (k n) -> p k n", n=512)
                            for f in range(2):
                                c = (2 * b + f) * P
                                for k in range(KD):
                                    last = nc.tensor.matmul(ps[b][:, f, :], weights[:, k, c:c + P], xT[:, k, :],
                                                            start=(k == 0), stop=(k == KD - 1))
                            last.then_inc(done[b], 1)
                    for b in range(2):
                        pe.wait_ge(hdn_made[b], 4 * e + 4)
                    for q in range(SLICES):
                        b, piece = q % 2, 2 * SLICES + q
                        pe.wait_ge(w_ready[piece % RING], 32 * e + 32)
                        pe.wait_ge(down_copied[b], 2 * e + q // 2)
                        weights = ring[:, piece % RING, :].rearrange("p (k n) -> p k n", n=256)
                        for d in range(2):
                            for f in range(NFT):
                                last = nc.tensor.matmul(down_ps[b][:, d, :], weights[:, f, d * P:(d + 1) * P],
                                                        hdn[:, f, :], start=(f == 0), stop=(f == NFT - 1))
                        last.then_inc(down_mm[q], 1)
                    pe.wait_ge(out_read, 4 * e)
                    turn_in(e + 1)
                    turn_out(e)

            @block.scalar
            def _(act):
                with act.Fori(0, NE) as e:
                    for n in range(UNITS):
                        q, b = n // 2, n % 2
                        act.wait_ge(gate_mm[b], 4 * e + q + 1)
                        act.wait_ge(hdn_made[b], 4 * e + q)
                        nc.scalar.activation(sil[:, b], gate_ps[b][:], ACT.Silu).then_inc(silu_done[b], 1)
                    for q in range(SLICES):
                        act.wait_ge(down_mm[q], e + 1)
                        nc.scalar.activation(outT[:, 2 * q:2 * q + 2, :], down_ps[q % 2][:], ACT.Copy)\
                          .then_inc(down_copied[q % 2], 1)

            @block.vector
            def _(dve):
                def copy_in(e):
                    for j in range(3):
                        dve.wait_ge(in_turned, 3 * e + j + 1)
                        if j == 2:
                            to, ps = xT[:, :, CS:TOK], turn_ps[0][:, 0:KD * CP].rearrange("p (k c) -> p k c", k=KD)
                        else:
                            to, ps = xT[:, 4 * j:4 * j + 4, 0:CS], turn_ps[j][:].rearrange("p (k c) -> p k c", k=4)
                        nc.vector.tensor_copy(to, ps).then_inc(in_read, 1)

                copy_in(0)
                with dve.Fori(0, NE) as e:
                    for n in range(UNITS):
                        q, b = n // 2, n % 2
                        dve.wait_ge(silu_done[b], 4 * e + q + 1)
                        dve.wait_ge(up_mm[b], 4 * e + q + 1)
                        if n == 0:
                            dve.wait_ge(down_mm[SLICES - 1], e)
                        nc.vector.tensor_tensor(hdn[:, 2 * n:2 * n + 2, :], sil[:, b], up_ps[b][:], ALU.mult)\
                          .then_inc(hdn_made[b], 1)
                    copy_in(e + 1)
                    dve.wait_ge(added, 32 * e)
                    for j in range(4):
                        dve.wait_ge(out_turned, 4 * e + j + 1)
                        x, half = 1 - j % 2, slice(j // 2 * 512, (j // 2 + 1) * 512)
                        to = (out_p, out_s)[x]
                        nc.vector.tensor_scalar(to[:, half], turn_ps[x][0:CAPS[x], :], gates[x][:, bass.ds(e, 1)], None,
                                                ALU.mult).then_inc(out_read, 1)


def stage_norm_out(nc, y, g, b, out):
    with ExitStack() as ctx:
        s = Stage(nc, ctx, "ln2")
        x_in, x_out = s.sb("x_in", [P, 2, D]), s.sb("x_out", [P, 2, D])
        g_all, b_all = s.sb("g_all", [P, D]), s.sb("b_all", [P, D])
        stats, mv, veps, rstd, mhalf = (s.sb(n, sh) for n, sh in (
            ("stats", [P, 2, 2, 6]), ("mv", [P, 2, 2]), ("veps", [P, 2]), ("rstd", [P, 2]), ("mhalf", [P, 1])))
        consts_in, half_made, var_eps, chain, var_ready = (s.sem(n) for n in (
            "consts_in", "half_made", "var_eps", "chain", "var_ready"))
        rstd_ready, x_ready, x_read, out_ready, stored = (s.sems(n, 2) for n in (
            "rstd_ready", "x_ready", "x_read", "out_ready", "stored"))
        with nc.Block() as block:
            @block.sync
            def _(sp):
                sp.dma_start(g_all[:], rows_of(g, D)).then_inc(consts_in, 16)
                sp.dma_start(b_all[:], rows_of(b, D)).then_inc(consts_in, 16)

                def load(t, u, r):
                    sp.wait_ge(x_read[u], r)
                    sp.dma_start(x_in[:, u], y[bass.ds(t * P, P), :]).then_inc(x_ready[u], 16)

                in_steps(sp, [(0, load)])

            @block.vector
            def _(dve):
                def measure(t, u, r):
                    dve.wait_ge(x_ready[u], 16 * r + 16)
                    for x in range(2):
                        nc.vector.bn_stats(stats[:, u, x, :], x_in[:, u, x * 512:(x + 1) * 512]).then_inc(chain, 1)
                    count = held(dve, 2 * t + 2)
                    dve.wait_ge(consts_in, 32)
                    dve.wait_ge(chain, count)
                    nc.vector.bn_aggr(mv[:, u], stats[:, u]).then_inc(var_ready, 1)

                def shift(t, u, r):
                    dve.wait_ge(out_ready[u], 2 * r + 1)
                    nc.vector.tensor_tensor(x_out[:, u], x_out[:, u], b_all[:], ALU.add).then_inc(out_ready[u], 1)

                def centre(t, u, r):
                    dve.wait_ge(stored[u], 16 * r)
                    dve.wait_ge(var_ready, t + 1)
                    dve.wait_ge(rstd_ready[u], r + 1)
                    nc.vector.tensor_scalar(x_out[:, u], x_in[:, u], mv[:, u, 0:1], rstd[:, u:u + 1], ALU.subtract,
                                            ALU.mult).then_inc(x_read[u], 1)

                dve.wait_ge(consts_in, 32)
                in_steps(dve, [(0, measure), (1, centre), (2, shift)])

            @block.gpsimd
            def _(pool):
                nc.gpsimd.memset(mhalf[:], -0.5).then_inc(half_made, 1)
                pool.wait_ge(half_made, 1)
                pool.wait_ge(consts_in, 32)

                def invert(t, u, r):
                    count = held(pool, t + 1)
                    pool.wait_ge(half_made, 1)
                    pool.wait_ge(var_ready, count)
                    nc.gpsimd.tensor_scalar(veps[:, u:u + 1], mv[:, u, 1:2], LN_EPS, None, ALU.add).then_inc(var_eps, 1)
                    pool.wait_ge(var_eps, t + 1)
                    nc.gpsimd.tensor_tensor(rstd[:, u:u + 1], veps[:, u:u + 1], mhalf[:], ALU.pow)\
                      .then_inc(rstd_ready[u], 1)

                def scale(t, u, r):
                    pool.wait_ge(x_read[u], r + 1)
                    nc.gpsimd.tensor_tensor(x_out[:, u], x_out[:, u], g_all[:], ALU.mult).then_inc(out_ready[u], 1)

                in_steps(pool, [(0, invert), (1, scale)])

            @block.scalar
            def _(act):
                def store(t, u, r):
                    act.wait_ge(out_ready[u], 2 * r + 2)
                    act.dma_start(out[bass.ds(t * P, P), :], x_out[:, u]).then_inc(stored[u], 16)

                in_steps(act, [(0, store)])
                for u in range(2):
                    act.wait_ge(stored[u], 16 * (NT // 2))


def build(nc, x, ln_in_g, ln_in_b, w_in, rpb, lb_fwd, lb_bwd, norm_g, w_na, w_hg, w_out, ln1_g, ln1_b, w_router,
          w_gate, w_up, w_down, ln2_g, ln2_b, out):
    def scratch(name, shape):
        return nc.dram_tensor(name, shape, F32).ap()

    xln, h, aT, o = scratch("xln", [T, D]), scratch("h", [T, IN_W]), scratch("aT", [NAW, T]), scratch("o", [T, HGW])
    mix, x1, y = scratch("mix", [T, D]), scratch("x1", [T, D]), scratch("y", [T, D])
    padded = nc.dram_tensor("padded", [NA_HEADS * (2 * KH - 1), GRID_W, 2 * GRID_W - 1], F32)
    with ExitStack() as ctx:
        s = Stage(nc, ctx, "main")
        ident = s.sb("ident", [P, P])
        stage_consts(nc, ident)
        with ExitStack() as bias:
            b = Stage(nc, bias, "bias")
            table = b.sb("table", [P, NA_HEADS, NROW, GRID_W])
            with ExitStack() as front:
                f = Stage(nc, front, "front")
                xT_hi, xT_lo = f.sb("xT_hi", [P, KD, T], F32R), f.sb("xT_lo", [P, KD, T], F32R)
                stage_norm_in(nc, ident, x, ln_in_g, ln_in_b, xln, xT_hi, xT_lo)
                wide = f.sb("wide", [NA_HEADS * (2 * KH - 1), 2 * GRID_W - 1])
                on_pool = [bias_pad(nc, rpb, padded.ap(), wide, f.sems("pad", 3)),
                           bias_tables(nc, padded, table, f.sems("table", 2))]
                stage_project(nc, w_in, h, xT_hi, xT_lo, on_pool)
            stage_attention(nc, ident, h, table, aT)
        stage_recurrence(nc, ident, h, lb_fwd, lb_bwd, o)
        stage_mix(nc, ident, h, aT, o, norm_g, w_na, w_hg, mix)
        gates = [s.sb(f"gates{n}", [CAPS[n], NE]) for n in range(2)]
        picks = [s.sb(f"picks{n}", [CAPS[n], NE + 1], U32) for n in range(2)]
        with ExitStack() as routing:
            affT = Stage(nc, routing, "route").sb("affT", [NE, T])
            stage_out(nc, ident, mix, xln, w_out, ln1_g, ln1_b, w_router, x1, y, affT)
            stage_choose(nc, ident, affT, gates, picks)
        stage_experts(nc, ident, x1, w_gate, w_up, w_down, gates, picks, y)
        stage_norm_out(nc, y, ln2_g, ln2_b, out)


def kernel(**inputs):
    import numpy as np
    import concourse.bacc as bacc
    from concourse import mybir as _mybir
    from concourse.bass_utils import run_bass_kernel_spmd

    arrays = {"x": np.concatenate([np.asarray(inputs["x_prompt"])[0], np.asarray(inputs["x_sample"])[0]], axis=0)}
    for name in ("ln_in_g", "ln_in_b", "w_in", "na_rpb", "hg_lb_fwd", "hg_lb_bwd", "hg_norm_g", "w_branch_na",
                 "w_branch_hg", "w_out", "ln1_g", "ln1_b", "w_router", "w_gate_e", "w_up_e", "w_down_e", "ln2_g",
                 "ln2_b"):
        a = np.asarray(inputs[name])
        if name == "na_rpb":
            arrays[name] = a[0]
        else:
            arrays[name] = a.reshape(-1) if a.size == a.shape[-1] else a.reshape(-1, a.shape[-1])
    nc = bacc.Bacc("TRN2", target_bir_lowering=False, num_devices=1)
    arrays = {f"in_{name}": np.ascontiguousarray(a) for name, a in arrays.items()}
    args = [nc.dram_tensor(name, a.shape, _mybir.dt.from_np(a.dtype), kind="ExternalInput").ap()
            for name, a in arrays.items()]
    args.append(nc.dram_tensor("out", [T, D], _mybir.dt.float32, kind="ExternalOutput").ap())
    build(nc, *args)
    got = run_bass_kernel_spmd(nc, [arrays], core_ids=[0]).results[0]["out"]
    return got[None, 0:SEQS[0][1]], got[None, SEQS[1][0]:]
```

```python
import math
from contextlib import ExitStack

import concourse.bass as bass
from concourse import mybir

F32 = mybir.dt.float32
F32R = mybir.dt.float32r
I32 = mybir.dt.int32
U32 = mybir.dt.uint32
U8 = mybir.dt.uint8
ACT = mybir.ActivationFunctionType
ALU = mybir.AluOpType
AX = mybir.AxisListType

P = 128
D = 1024
KD = D // P
SEQS = ((0, 256), (256, 1024))
T = 1280
NT = T // P
GRID_W = 64
NA_HEADS, NA_DIM = 8, 64
KH, KW = 8, 16
HG_HEADS = 4
NAW = NA_HEADS * NA_DIM
HGW = HG_HEADS * P
IN_W = 3 * NAW + 5 * HGW + 2 * D
COL_Q, COL_K, COL_V = 0, NAW, 2 * NAW
COL_HQ, COL_ZF, COL_ZB, COL_I, COL_G = (3 * NAW + n * HGW for n in range(5))
COL_GATE = 3 * NAW + 5 * HGW
NE = 16
CAPS = (2 * 256 // NE, 2 * 1024 // NE)
TOK = CAPS[0] + CAPS[1]
FF = 2 * D
NFT = FF // P
ALPHA = 2 ** 0.25
LN_EPS, RMS_EPS = 1e-5, 1e-6
NEG_BIG = -1e30
F_MIN = 1e-30
SLAB = 512
NSLAB = IN_W // SLAB


class Steps:

    def __init__(self, per):
        self.per, self.base, self.n = per, 0, 0

    def round(self, r):
        assert self.n in (0, self.per), (self.n, self.per)
        self.base, self.n = r * self.per, 0

    def next(self):
        self.n += 1
        return self.base + self.n


class Stage:

    def __init__(self, nc, ctx, name):
        self.nc, self.ctx, self.name = nc, ctx, name
        self.semaphores = []
        ctx.callback(self.release)

    def sb(self, name, shape, dt=F32):
        return self.ctx.enter_context(self.nc.sbuf_tensor(f"{self.name}_{name}", shape, dt))

    def ps(self, name, shape, dt=F32):
        return self.ctx.enter_context(self.nc.psum_tensor(f"{self.name}_{name}", shape, dt))

    def sem(self, name):
        self.semaphores.append(self.nc.alloc_semaphore(f"{self.name}_{name}"))
        return self.semaphores[-1]

    def sems(self, name, n):
        return [self.sem(f"{name}{i}") for i in range(n)]

    def release(self):
        if self.semaphores:
            self.nc.clear_and_free_semaphores(self.semaphores)
            self.nc.all_engine_barrier()


def held(eng, count):
    return count if isinstance(count, int) else eng.to_reg(count)


def in_steps(eng, parts):
    last = max(lag for lag, _ in parts)

    def step(i, u):
        for lag, part in parts:
            if not isinstance(i, int) or 0 <= 2 * i + u - lag < NT:
                part(2 * i + u - lag, (u - lag) % 2, i + (u - lag) // 2)

    first = (last + 1) // 2
    for n in range(2 * first):
        step(n // 2, n % 2)
    with eng.Fori(first, NT // 2) as i:
        for u in range(2):
            step(i, u)
    for n in range(NT, NT + last):
        step(n // 2, n % 2)


def rows_of(vector_ap, n):
    return bass.AP(vector_ap.tensor, offset=vector_ap.offset, ap=[[0, P], [1, n]])


def stage_consts(nc, ident):
    with ExitStack() as ctx:
        s = Stage(nc, ctx, "const")
        zeroed, made = s.sem("zeroed"), s.sem("made")
        with nc.Block() as block:
            @block.gpsimd
            def _(pool):
                nc.gpsimd.memset(ident[:], 0.0).then_inc(zeroed, 1)
                pool.wait_ge(zeroed, 1)
                nc.gpsimd.affine_select(out=ident[:], in_=ident[:], compare_op=ALU.not_equal, fill=1.0,
                                        base=0, pattern=[[-1, P]], channel_multiplier=1).then_inc(made, 1)
                pool.wait_ge(made, 1)


def stage_norm_in(nc, ident, x, g, b, xln, xT_hi, xT_lo):
    with ExitStack() as ctx:
        s = Stage(nc, ctx, "ln0")
        x_in = s.sb("x_in", [P, 2, D])
        y = s.sb("y", [P, 4, D])
        g_all, b_all = s.sb("g_all", [P, D]), s.sb("b_all", [P, D])
        stats, mv = s.sb("stats", [P, 2, 2, 6]), s.sb("mv", [P, 2, 2])
        rstd, veps, minus_half = s.sb("rstd", [P, 2]), s.sb("veps", [P, 2]), s.sb("mhalf", [P, 1])
        tp = [s.ps(f"tp{u}", [P, D]) for u in range(2)]
        consts_in, half_made, var_eps, chain = (s.sem(n) for n in ("consts_in", "half_made", "var_eps", "chain"))
        var_ready, hi_done, scaled = s.sem("var_ready"), s.sem("hi_done"), s.sems("scaled", 2)
        rstd_ready, x_ready, x_read, y_ready, y_stored, y_turned, lo_done = (s.sems(n, 2) for n in (
            "rstd_ready", "x_ready", "x_read", "y_ready", "y_stored", "y_turned", "lo_done"))
        with nc.Block() as block:
            @block.sync
            def _(sp):
                sp.dma_start(g_all[:], rows_of(g, D)).then_inc(consts_in, 16)
                sp.dma_start(b_all[:], rows_of(b, D)).then_inc(consts_in, 16)

                def load(t, u, r):
                    sp.wait_ge(x_read[u], r)
                    sp.dma_start(x_in[:, u], x[bass.ds(t * P, P), :]).then_inc(x_ready[u], 16)

                in_steps(sp, [(0, load)])

            @block.vector
            def _(dve):
                dve.wait_ge(consts_in, 32)

                def measure(t, u, r):
                    dve.wait_ge(x_ready[u], 16 * r + 16)
                    for x in range(2):
                        nc.vector.bn_stats(stats[:, u, x, :], x_in[:, u, x * 512:(x + 1) * 512]).then_inc(chain, 1)
                    count = held(dve, 2 * t + 2)
                    dve.wait_ge(consts_in, 32)
                    dve.wait_ge(chain, count)
                    nc.vector.bn_aggr(mv[:, u], stats[:, u]).then_inc(var_ready, 1)

                def centre(t, u, r):
                    dve.wait_ge(scaled[u], r)
                    dve.wait_ge(var_ready, t + 1)
                    dve.wait_ge(rstd_ready[u], r + 1)
                    nc.vector.tensor_scalar(y[:, u], x_in[:, u], mv[:, u, 0:1], rstd[:, u:u + 1], ALU.subtract,
                                            ALU.mult).then_inc(x_read[u], 1)

                def shift(t, u, r):
                    dve.wait_ge(scaled[u], r + 1)
                    nc.vector.tensor_tensor(y[:, 2 + u], y[:, 2 + u], b_all[:], ALU.add).then_inc(y_ready[u], 1)

                def split(t, u, r):
                    dve.wait_ge(hi_done, t + 1)
                    for x in range(2):
                        last = nc.vector.tensor_tensor(
                            xT_lo[:, 4 * x:4 * x + 4, bass.ds(t * P, P)],
                            tp[u][:, 512 * x:512 * x + 512].rearrange("p (k c) -> p k c", k=4),
                            xT_hi[:, 4 * x:4 * x + 4, bass.ds(t * P, P)].bitcast(F32), ALU.subtract)
                    last.then_inc(lo_done[u], 1)

                in_steps(dve, [(1, centre), (0, measure), (2, shift), (3, split)])

            @block.gpsimd
            def _(pool):
                nc.gpsimd.memset(minus_half[:], -0.5).then_inc(half_made, 1)
                pool.wait_ge(half_made, 1)
                pool.wait_ge(consts_in, 32)

                def invert(t, u, r):
                    count = held(pool, t + 1)
                    pool.wait_ge(half_made, 1)
                    pool.wait_ge(var_ready, count)
                    nc.gpsimd.tensor_scalar(veps[:, u:u + 1], mv[:, u, 1:2], LN_EPS, None, ALU.add).then_inc(var_eps, 1)
                    pool.wait_ge(var_eps, t + 1)
                    nc.gpsimd.tensor_tensor(rstd[:, u:u + 1], veps[:, u:u + 1], minus_half[:], ALU.pow)\
                      .then_inc(rstd_ready[u], 1)

                def scale(t, u, r):
                    pool.wait_ge(y_stored[u], 16 * r)
                    pool.wait_ge(y_turned[u], r)
                    pool.wait_ge(x_read[u], r + 1)
                    nc.gpsimd.tensor_tensor(y[:, 2 + u], y[:, u], g_all[:], ALU.mult).then_inc(scaled[u], 1)

                in_steps(pool, [(0, invert), (1, scale)])

            @block.tensor
            def _(pe):
                def turn(t, u, r):
                    pe.wait_ge(y_ready[u], r + 1)
                    pe.wait_ge(lo_done[u], r)
                    for k in range(KD):
                        last = nc.tensor.transpose(tp[u][:, k * P:(k + 1) * P], y[:, 2 + u, k * P:(k + 1) * P],
                                                   ident[:])
                    last.then_inc(y_turned[u], 1)

                in_steps(pe, [(2, turn)])

            @block.scalar
            def _(act):
                def split(t, u, r):
                    act.wait_ge(y_ready[u], r + 1)
                    act.dma_start(xln[bass.ds(t * P, P), :], y[:, 2 + u]).then_inc(y_stored[u], 16)
                    act.wait_ge(y_turned[u], r + 1)
                    for x in range(2):
                        last = nc.scalar.activation(
                            xT_hi[:, 4 * x:4 * x + 4, bass.ds(t * P, P)],
                            tp[u][:, 512 * x:512 * x + 512].rearrange("p (k c) -> p k c", k=4), ACT.Copy)
                    last.then_inc(hi_done, 1)

                in_steps(act, [(2, split)])
                for u in range(2):
                    act.wait_ge(y_stored[u], 16 * (NT // 2))


def stage_project(nc, w_in, h, xT_hi, xT_lo, bias_on_pool):
    NB = 5
    with ExitStack() as ctx:
        s = Stage(nc, ctx, "proj")
        raw = s.sb("raw", [P, 2, 4, SLAB])
        w_hi, w_lo = s.sb("w_hi", [P, 2, KD, SLAB], F32R), s.sb("w_lo", [P, 2, KD, SLAB], F32R)
        out = s.sb("out", [P, NB, SLAB])
        acc = [s.ps(f"acc{n}", [P, SLAB]) for n in range(NB)]
        w_ready, hi_done, lo_done = s.sems("w_ready", 2), s.sems("hi_done", 2), s.sems("lo_done", 2)
        mm_done, slab_done = s.sems("mm_done", NB), s.sems("slab_done", 2)
        copied, stored = s.sems("copied", NB), s.sems("stored", NB)
        w_view = w_in.rearrange("(k p) n -> p k n", p=P)
        with nc.Block() as block:
            @block.gpsimd
            def _(pool):
                for part in bias_on_pool:
                    part(pool)

            @block.sync
            def _(sp):
                with sp.Fori(0, NSLAB) as j:
                    for v in range(2):
                        sp.wait_ge(lo_done[v], j)
                        sp.dma_start(raw[:, v], w_view[:, 4 * v:4 * v + 4, bass.ds(j * SLAB, SLAB)])\
                          .then_inc(w_ready[v], 16)

            @block.scalar
            def _(act):
                def split(j, u, uses):
                    act.wait_ge(slab_done[u], uses)
                    for v in range(2):
                        act.wait_ge(w_ready[v], 16 * j + 16)
                        nc.scalar.activation(w_hi[:, u, 4 * v:4 * v + 4, :], raw[:, v], ACT.Copy)\
                          .then_inc(hi_done[v], 1)

                def slab(i, u, last):
                    j = 2 * i + u
                    for t in range(NT):
                        n, r = t % NB, 2 * j + t // NB
                        if t == 4 and not last:
                            split(j + 1, 1 - u, i + u)
                        if t % 2 == 0:
                            act.wait_ge(mm_done[n], j + 1 if n == NB - 1 else r + 1)
                            act.wait_ge(stored[n], 16 * r)
                            nc.scalar.activation(out[:, n, :], acc[n][:], ACT.Copy).then_inc(copied[n], 1)
                        act.wait_ge(copied[n], r + 1)
                        act.dma_start(h[t * P:(t + 1) * P, bass.ds(j * SLAB, SLAB)], out[:, n, :])\
                           .then_inc(stored[n], 16)

                split(0, 0, 0)
                with act.Fori(0, NSLAB // 2 - 1) as i:
                    slab(i, 0, False)
                    slab(i, 1, False)
                slab(NSLAB // 2 - 1, 0, False)
                slab(NSLAB // 2 - 1, 1, True)
                for n in range(NB):
                    act.wait_ge(stored[n], 16 * 2 * NSLAB)

            @block.vector
            def _(dve):
                def split(j, u):
                    for v in range(2):
                        dve.wait_ge(hi_done[v], j + 1)
                        nc.vector.tensor_tensor(w_lo[:, u, 4 * v:4 * v + 4, :], raw[:, v],
                                                w_hi[:, u, 4 * v:4 * v + 4, :].bitcast(F32), ALU.subtract)\
                          .then_inc(lo_done[v], 1)

                def slab(i, u, last):
                    j = 2 * i + u
                    for t in range(NT):
                        n, r = t % NB, 2 * j + t // NB
                        if t == 4 and not last:
                            split(j + 1, 1 - u)
                        if t % 2:
                            if t == NT - 1:
                                dve.wait_ge(slab_done[u], i + 1)
                            else:
                                dve.wait_ge(mm_done[n], r + 1)
                            dve.wait_ge(stored[n], 16 * r)
                            nc.vector.tensor_copy(out[:, n, :], acc[n][:]).then_inc(copied[n], 1)

                split(0, 0)
                with dve.Fori(0, NSLAB // 2 - 1) as i:
                    slab(i, 0, False)
                    slab(i, 1, False)
                slab(NSLAB // 2 - 1, 0, False)
                slab(NSLAB // 2 - 1, 1, True)

            @block.tensor
            def _(pe):
                with pe.Fori(0, NSLAB // 2) as i:
                    for u in range(2):
                        j = 2 * i + u
                        for t in range(NT):
                            n, r = t % NB, 2 * j + t // NB
                            pe.wait_ge(copied[n], r)
                            for k in range(KD):
                                if t == 0 and k % 4 == 0:
                                    pe.wait_ge(lo_done[k // 4], j + 1)
                                tile = slice(t * P, (t + 1) * P)
                                nc.tensor.matmul(acc[n][:], xT_hi[:, k, tile], w_hi[:, u, k, :],
                                                 start=(k == 0), stop=False)
                                nc.tensor.matmul(acc[n][:], xT_hi[:, k, tile], w_lo[:, u, k, :],
                                                 start=False, stop=False)
                                last = nc.tensor.matmul(acc[n][:], xT_lo[:, k, tile], w_hi[:, u, k, :],
                                                        start=False, stop=(k == KD - 1))
                            last.then_inc(slab_done[u] if t == NT - 1 else mm_done[n], 1)


NROW = 14


def attention_items():
    items = []
    for first, tokens in SEQS:
        rows = tokens // GRID_W
        kh = min(KH, rows)
        for r0 in range(0, rows, 2):
            s0, s1 = (min(max(r - kh // 2, 0), rows - kh) for r in (r0, r0 + 1))
            assert s0 % 2 == 0 and s1 - s0 in (0, 1)
            items.append(((first + r0 * GRID_W) // P, (first + s0 * GRID_W) // P,
                          (kh + s1 - s0) * GRID_W, s0 - r0 + 6, s1 != s0))
    return items


def bias_pad(nc, rpb, padded, sb, sems):
    zeroed, read, written = sems
    W = 2 * GRID_W - 1
    n = NA_HEADS * (2 * KH - 1)

    def on_pool(pool):
        nc.gpsimd.memset(sb[0:n, :], 0.0).then_inc(zeroed, 1)
        pool.wait_ge(zeroed, 1)
        pool.dma_start(sb[0:n, GRID_W - KW:GRID_W + KW - 1], rpb.rearrange("h r c -> (h r) c")).then_inc(read, 16)
        pool.wait_ge(read, 16)
        pool.dma_start(padded, sb[0:n, :].unsqueeze(1).to_broadcast([n, GRID_W, W])).then_inc(written, 16)
        pool.wait_ge(written, 16)
    return on_pool


def bias_tables(nc, padded, table, sems):
    loaded, masked = sems
    W = 2 * GRID_W - 1

    def on_pool(pool):
        for head in range(NA_HEADS):
            for half in range(2):
                row = head * (2 * KH - 1) + 1 - half
                src = bass.AP(padded, offset=row * GRID_W * W + GRID_W - 1,
                              ap=[[W - 1, GRID_W], [GRID_W * W, NROW], [1, GRID_W]])
                pool.dma_start(table[half * GRID_W:(half + 1) * GRID_W, head], src).then_inc(loaded, 16)
        pool.wait_ge(loaded, 16 * 2 * NA_HEADS)
        w = GRID_W - KW
        n = 0
        for half in range(2):
            rows = table[half * GRID_W:(half + 1) * GRID_W].rearrange("p h n c -> p (h n) c")
            nc.gpsimd.affine_select(out=rows[:, :, 0:w], in_=rows[:, :, 0:w], compare_op=ALU.is_ge, fill=NEG_BIG,
                                    base=KW // 2, pattern=[[0, NA_HEADS * NROW], [1, w]],
                                    channel_multiplier=-1).then_inc(masked, 1)
            n += 1
            pool.wait_ge(masked, n)
            nc.gpsimd.affine_select(out=rows[:, :, KW:], in_=rows[:, :, KW:], compare_op=ALU.is_gt, fill=NEG_BIG,
                                    base=KW // 2 - KW, pattern=[[0, NA_HEADS * NROW], [-1, w]],
                                    channel_multiplier=1).then_inc(masked, 1)
            n += 1
            pool.wait_ge(masked, n)
    return on_pool


def stage_attention(nc, ident, h, table, aT):
    items = [(t, k0, keys, row, two, u) for t, k0, keys, row, two in attention_items() for u in range(2)]
    N = len(items)
    SCALE = NA_DIM ** -0.5
    MAXK = (KH + 1) * GRID_W
    SLOTS = 4
    assert N % SLOTS == 0
    with ExitStack() as ctx:
        s = Stage(nc, ctx, "na")
        qkv = s.sb("qkv", [P, 2, 3, NT, P])
        qz = s.sb("qz", [P, 2, 2, T])
        kT = s.sb("kT", [P, 2, T])
        sc = s.sb("sc", [P, SLOTS, MAXK])
        pT = s.sb("pT", [P, 2, 5 * P])
        out = s.sb("out", [P, 2, T])
        nmax, total, inv = (s.sb(name, [P, SLOTS]) for name in ("nmax", "total", "inv"))
        s_ps = [s.ps(f"s{m}", [P, 2, 512]) for m in range(2)]
        t_ps = s.ps("t", [P, 2 * 512])
        o_ps = [s.ps(f"o{m}", [P, 512]) for m in range(2)]
        loaded, stored, slot_done = s.sems("loaded", 2), s.sems("stored", 2), s.sems("slot_done", 2)
        qz_zeroed, turned, turned_read = s.sem("qz_zeroed"), s.sem("turned"), s.sem("turned_read")
        qk_done, biased, edges, maxed, exp_done = (s.sem(n) for n in ("qk_done", "biased", "edges", "maxed", "exp"))
        inverted, normed, p_turned, p_copied = (s.sem(n) for n in ("inverted", "normed", "p_turned", "p_copied"))
        pv_done, o_copied = s.sem("pv_done"), s.sem("o_copied")
        groups = [(x, a, min(4, NT - a)) for x in range(2) for a in range(0, NT, 4)]
        G = len(groups)

        def in_bank(m):
            return s_ps[m % 4 // 2][:, m % 2, :]

        n_two = sum(it[4] for it in items)
        with nc.Block() as block:
            @block.sync
            def _(sp):
                def load(hp, w, i):
                    sp.wait_ge(slot_done[w], i)
                    for x, col in enumerate((COL_Q, COL_K, COL_V)):
                        sp.dma_start(qkv[:, w, x],
                                     h[:, bass.ds(hp * P + col, P)].rearrange("(t p) c -> p t c", p=P))\
                          .then_inc(loaded[w], 16)

                with sp.Fori(0, 2) as i:
                    for w in range(2):
                        load(2 * i + w, w, i)
                load(0, 0, 2)
                sp.wait_ge(loaded[0], 48 * 3)

            @block.gpsimd
            def _(pool):
                with pool.Fori(0, 2) as i:
                    for w in range(2):
                        hp = 2 * i + w
                        pool.wait_ge(o_copied, (hp + 1) * NT)
                        pool.dma_start(aT[bass.ds(hp * P, P), :], out[:, w]).then_inc(stored[w], 16)
                for w in range(2):
                    pool.wait_ge(stored[w], 32)

            @block.tensor
            def _(pe):
                def scores(g, hp, n, w):
                    t, k0, keys, row, two, u = items[n]
                    if n == 0:
                        pe.wait_ge(turned_read, (hp + 1) * G)
                    if n >= 2:
                        pe.wait_ge(biased, g - 1)
                    half = keys // 2
                    for a in range(2):
                        last = nc.tensor.matmul(s_ps[n % 2][:, a, 0:half], qz[:, w, u, t * P:(t + 1) * P],
                                                kT[:, w, k0 * P + a * half:k0 * P + (a + 1) * half],
                                                start=True, stop=True)
                    last.then_inc(qk_done, 1)

                def turn(g, n):
                    keys = items[n][2]
                    pe.wait_ge(normed, g + 1)
                    if n >= 1:
                        pe.wait_ge(p_copied, g)
                    for c in range(0, keys, P):
                        m = min(P, keys - c)
                        last = nc.tensor.transpose(t_ps[0:m, c:c + P], sc[:, n % SLOTS, c:c + m], ident[:])
                    last.then_inc(p_turned, 1)

                def values(g, hp, n, i, w):
                    t, k0, keys, row, two, u = items[n]
                    pe.wait_ge(p_copied, g + 1)
                    if n // 2 >= 2:
                        pe.wait_ge(o_copied, hp * NT + n // 2 - 1)
                    for c in range(0, keys, P):
                        m = min(P, keys - c)
                        last = nc.tensor.matmul(o_ps[(n // 2) % 2][u * 64:u * 64 + 64, 0:P],
                                                qkv[0:m, w, 2, k0 + c // P, u * 64:u * 64 + 64],
                                                pT[0:m, n % 2, c:c + P], start=(c == 0), stop=(c + P >= keys))
                    last.then_inc(slot_done[w] if n == N - 1 else pv_done, 1)

                def turn_in(p, w, use, first, count):
                    if first == 0:
                        pe.wait_ge(loaded[w], 48 * use + 48)
                        pe.wait_ge(biased, p * N)
                    for m in range(first, first + count):
                        x, a, tiles = groups[m]
                        if m >= 4:
                            pe.wait_ge(turned_read, p * G + m - 3)
                        for c in range(tiles):
                            last = nc.tensor.transpose(in_bank(m)[:, c * P:(c + 1) * P], qkv[:, w, x, a + c, :],
                                                       ident[:])
                        last.then_inc(turned, 1)

                pe.wait_ge(qz_zeroed, 1)
                turn_in(0, 0, 0, 0, G)
                with pe.Fori(0, 2) as i:
                    for w in range(2):
                        hp = 2 * i + w
                        g0 = hp * N
                        for n in range(N + 4):
                            if n < N:
                                scores(g0 + n, hp, n, w)
                            if 3 <= n < N + 3:
                                turn(g0 + n - 3, n - 3)
                            if n >= 4:
                                values(g0 + n - 4, hp, n - 4, i, w)
                            if n == N:
                                turn_in(hp + 1, 1 - w, i + w, 0, 4)
                            if n == N + 1:
                                turn_in(hp + 1, 1 - w, i + w, 4, G - 4)

            @block.vector
            def _(dve):
                def bias(g, hp, n, n_before):
                    t, k0, keys, row, two, u = items[n]
                    half = keys // 2
                    dve.wait_ge(qk_done, g + 1)
                    if n >= SLOTS:
                        dve.wait_ge(p_turned, g - SLOTS + 1)
                    nc.vector.scalar_tensor_tensor(
                        sc[:, n % SLOTS, 0:keys].rearrange("p (a c) -> p a c", a=2), s_ps[n % 2][:, :, 0:half], SCALE,
                        table[:, bass.ds(2 * hp + u, 1), row:row + keys // GRID_W, :]
                        .rearrange("p h n c -> p (h n c)").rearrange("p (a c) -> p a c", a=2),
                        ALU.mult, ALU.add).then_inc(biased, 1)
                    dve.wait_ge(biased, g + 1)
                    if two:
                        nc.vector.memset(sc[0:64, n % SLOTS, KH * GRID_W:keys], NEG_BIG).then_inc(edges, 1)
                        nc.vector.memset(sc[64:128, n % SLOTS, 0:GRID_W], NEG_BIG).then_inc(edges, 1)
                        dve.wait_ge(edges, 2 * (hp * n_two + n_before + 1))
                    nc.vector.tensor_reduce(nmax[:, n % SLOTS:n % SLOTS + 1], sc[:, n % SLOTS, 0:keys], AX.X, ALU.max,
                                            negate=True).then_inc(maxed, 1)

                def norm(g, n):
                    keys = items[n][2]
                    dve.wait_ge(exp_done, g + 1)
                    one = slice(n % SLOTS, n % SLOTS + 1)
                    nc.vector.reciprocal(inv[:, one], total[:, one]).then_inc(inverted, 1)
                    dve.wait_ge(inverted, g + 1)
                    nc.vector.tensor_scalar(sc[:, n % SLOTS, 0:keys], sc[:, n % SLOTS, 0:keys], inv[:, one], None,
                                            ALU.mult).then_inc(normed, 1)

                nc.vector.memset(qz[:], 0.0).then_inc(qz_zeroed, 1)
                with dve.Fori(0, 4) as hp:
                    for n in range(N + 2):
                        if n < N:
                            bias(hp * N + n, hp, n, sum(it[4] for it in items[:n]))
                        if n >= 2:
                            norm(hp * N + n - 2, n - 2)

            @block.scalar
            def _(act):
                def exp(g, n):
                    keys = items[n][2]
                    act.wait_ge(maxed, g + 1)
                    nc.scalar.activation(sc[:, n % SLOTS, 0:keys], sc[:, n % SLOTS, 0:keys], ACT.Exp,
                                         bias=nmax[:, n % SLOTS:n % SLOTS + 1],
                                         accum_out=total[:, n % SLOTS:n % SLOTS + 1]).then_inc(exp_done, 1)

                def take_in(p, w, first, count):
                    for m in range(first, first + count):
                        x, a, tiles = groups[m]
                        act.wait_ge(turned, p * G + m + 1)
                        src, cols = in_bank(m)[:, 0:tiles * P], slice(a * P, (a + tiles) * P)
                        if x == 0:
                            nc.scalar.activation(qz[0:64, w, 0, cols], src[0:64], ACT.Copy)
                            last = nc.scalar.activation(qz[64:128, w, 1, cols], src[64:128], ACT.Copy)
                        else:
                            last = nc.scalar.activation(kT[:, w, cols], src, ACT.Copy)
                        last.then_inc(turned_read, 1)

                act.wait_ge(qz_zeroed, 1)
                take_in(0, 0, 0, G)
                with act.Fori(0, 2) as i:
                    for w in range(2):
                        hp = 2 * i + w
                        g0 = hp * N
                        act.wait_ge(stored[w], 16 * i)
                        for n in range(N + 6):
                            if 4 <= n < N + 4:
                                m = n - 4
                                act.wait_ge(p_turned, g0 + m + 1)
                                if m >= 2:
                                    act.wait_ge(pv_done, hp * (N - 1) + m - 1)
                                keys = items[m][2]
                                full = keys // P * P
                                last = nc.scalar.activation(pT[:, m % 2, 0:full], t_ps[:, 0:full], ACT.Copy)
                                if keys > full:
                                    last = nc.scalar.activation(pT[0:keys - full, m % 2, full:full + P],
                                                                t_ps[0:keys - full, full:full + P], ACT.Copy)
                                last.then_inc(p_copied, 1)
                            if 1 <= n < N + 1:
                                exp(g0 + n - 1, n - 1)
                            if n == N + 1:
                                take_in(hp + 1, 1 - w, 0, 4)
                            if n == N + 2:
                                take_in(hp + 1, 1 - w, 4, G - 4)
                            if n >= 6 and n % 2 == 1:
                                m = n - 6
                                if m == N - 1:
                                    act.wait_ge(slot_done[w], i + 1)
                                else:
                                    act.wait_ge(pv_done, hp * (N - 1) + m + 1)
                                t = items[m][0]
                                nc.scalar.activation(out[:, w, t * P:(t + 1) * P], o_ps[(m // 2) % 2][:, 0:P],
                                                     ACT.Copy).then_inc(o_copied, 1)


LEVELS = int(math.log2(P))
CHUNK_GROUPS = [(a, min(4, NT - a)) for a in range(0, NT, 4)]
LN_SPLIT = 2.0 ** -60


def stage_recurrence(nc, ident, h, lb_fwd, lb_bwd, o):
    assert all(first % P == 0 and tokens % P == 0 for first, tokens in SEQS)
    starts = {first // P for first, _ in SEQS}
    ends = {(first + tokens) // P - 1 for first, tokens in SEQS}
    NG = len(CHUNK_GROUPS)
    R = 2 + LEVELS
    NL = 1 + LEVELS
    WS = 3
    NI = 3 * NG
    assert R % WS == 0
    SETUP, PER = 6 + 3 * LEVELS, 3 * 2
    with ExitStack() as ctx:
        s = Stage(nc, ctx, "hg")
        raw = s.sb("raw", [P, 3, NT, P])
        v = s.sb("v", [P, NT, HGW])
        sgq, ksum = s.sb("sgq", [P, T]), s.sb("ksum", [P, T])
        qT, k = s.sb("qT", [P, 2, T]), s.sb("k", [P, 2, 2, T])
        f, lf = s.sb("f", [P, 2, T]), s.sb("lf", [P, 2, T])
        E = s.sb("E", [P, 2, NT, P + 1])
        W = s.sb("W", [P, WS, 2, T])
        qi = s.sb("qi", [P, 2, T])
        kiT = s.sb("kiT", [P, 2, NT, P])
        decay = s.sb("decay", [P, 2, NT])
        S = s.sb("S", [P, 2, NT, P])
        A = s.sb("A", [P, T])
        out = s.sb("out", [P, NT, P])
        diag = s.sb("diag", [P, 4, P])
        mask = s.sb("mask", [P, LEVELS, 4 * P], U8)
        cols_i, rows_i, xor_i = (s.sb(n, [P, 4 * P], I32) for n in ("cols_i", "rows_i", "xor_i"))
        below = s.sb("below", [P, 4 * P])
        lb, omlb = s.sb("lb", [P, 2, HG_HEADS]), s.sb("omlb", [P, 2, HG_HEADS])
        lb_e, lb_r = s.sb("lb_e", [P, 2, HG_HEADS]), s.sb("lb_r", [P, 2, HG_HEADS])
        tp = [s.ps(f"tp{m}", [P, 512]) for m in range(2)]
        sp_ps = [s.ps(f"s{m}", [P, 512]) for m in range(2)]
        in_ps = tp + sp_ps
        l_ps = [s.ps(f"l{m}", [P, 512]) for m in range(NG)]
        (raw_in, v_in, lb_in, iota_done, in_turned, in_read, sg_done, q_done, z_done, clamped, ln_done,
         scanned, dec_done, pool_d, dve_d, exp_done, w_ready, qi_done, ki_turned, ki_copied, l_mm, a_done,
         ds_mm, s_made, o_mm, o_copied, stored, chain, lb_ready) = (s.sem(n) for n in (
             "raw_in", "v_in", "lb_in", "iota_done", "in_turned", "in_read", "sg_done", "q_done", "z_done",
             "clamped", "ln_done", "scanned", "dec_done", "pool_d", "dve_d", "exp_done", "w_ready", "qi_done",
             "ki_turned", "ki_copied", "l_mm", "a_done", "ds_mm", "s_made", "o_mm", "o_copied", "stored",
             "chain", "lb_ready"))
        in_groups = [(x, a, n) for x in range(3) for a, n in CHUNK_GROUPS]
        ki_groups = [(0, a, n) for a, n in CHUNK_GROUPS] + [(1, a, n) for a, n in reversed(CHUNK_GROUPS)]
        made = [sum(c not in (ends, starts)[d] for d, a, n in ki_groups[:m + 1] for c in range(a, a + n))
                for m in range(2 * NG)]
        NS = made[-1]
        e_to = E[:, :, :, 0:P]
        e_with = E[:, :, :, 1:P + 1]

        def halves(view, m, side):
            return view.rearrange("p c (b h j) -> p c b h j", h=2, j=m)[:, :, :, side, :]

        def middle(d, m):
            return E[:, d, :, m:P:2 * m].unsqueeze(3).to_broadcast([P, NT, P // (2 * m), m])

        def chunked(view):
            return view.rearrange("p (c t) -> p c t", t=P)

        def exponents(r):
            z, y = (chunked(W[:, r % WS, x, :]) for x in range(2))
            last = [E[:, d, :, P:P + 1].to_broadcast([P, NT, P]) for d in range(2)]
            if r == 0:
                return [(y, last[0], e_with[:, 0])]
            if r == 1:
                return [(z, last[1], e_to[:, 1])]
            m = P >> (r - 1)
            return [(halves(y, m, 0), middle(0, m), halves(e_with[:, 0], m, 0)),
                    (halves(y, m, 1), halves(e_to[:, 1], m, 1), middle(1, m)),
                    (halves(z, m, 0), middle(1, m), halves(e_to[:, 1], m, 0)),
                    (halves(z, m, 1), halves(e_with[:, 0], m, 1), middle(0, m))]

        def wait_slot(eng, hd, r):
            if r < WS:
                eng.wait_ge(l_mm, hd * NL * NG)
            elif r < WS + 2:
                eng.wait_ge(ki_turned, hd * 2 * NG + (r - WS + 1) * NG)
                eng.wait_ge(qi_done, hd * 2 + r - WS + 1)
            else:
                eng.wait_ge(l_mm, (hd * NL + r - WS) * NG)

        with nc.Block() as block:
            @block.sync
            def _(sp):
                with nc.allow_non_contiguous_dma(reason="512 lower bounds, one per partition and head"):
                    for d, src in enumerate((lb_fwd, lb_bwd)):
                        sp.dma_start(lb[:, d, :], src.rearrange("(h p) -> p h", p=P)).then_inc(lb_in, 16)

                def load(p):
                    sp.wait_ge(in_turned, p * NI)
                    for x, col in enumerate((COL_HQ, COL_ZF, COL_ZB)):
                        sp.dma_start(raw[:, x], h[:, bass.ds(p % HG_HEADS * P + col, P)]
                                     .rearrange("(t p) c -> p t c", p=P)).then_inc(raw_in, 16)

                load(0)
                sp.dma_start(v[:], h[:, COL_I:COL_I + HGW].rearrange("(t p) c -> p t c", p=P)).then_inc(v_in, 16)
                with sp.Fori(0, HG_HEADS) as hd:
                    load(hd + 1)
                    count = held(sp, (hd + 1) * NG)
                    sp.wait_ge(v_in, 16)
                    sp.wait_ge(o_copied, count)
                    sp.dma_start(o[:, bass.ds(hd * P, P)].rearrange("(t p) c -> p t c", p=P), out[:])\
                      .then_inc(stored, 16)
                sp.wait_ge(raw_in, 48 * (HG_HEADS + 1))
                sp.wait_ge(stored, 16 * HG_HEADS)

            @block.gpsimd
            def _(pool):
                nc.gpsimd.iota(cols_i[:], pattern=[[0, 4], [1, P]], base=0, channel_multiplier=0).then_inc(iota_done, 1)
                nc.gpsimd.iota(rows_i[:], pattern=[[0, 4 * P]], base=0, channel_multiplier=1).then_inc(iota_done, 1)

                def prepare(p, w):
                    pool.wait_ge(sg_done, p + 1)
                    nc.gpsimd.tensor_tensor(qT[:, w], qT[:, w], sgq[:], ALU.mult)
                    pool.wait_ge(chain, SETUP + p * PER + PER)
                    nc.gpsimd.tensor_tensor(ksum[:], k[:, w, 0], k[:, w, 1], ALU.add).then_inc(q_done, 1)

                def difference(hd, r):
                    pool.wait_ge(scanned, hd * 2 + min(r + 1, 2))
                    wait_slot(pool, hd, r)
                    for to, a, b in exponents(r)[:3]:
                        last = nc.gpsimd.tensor_tensor(to, a, b, ALU.subtract)
                    last.then_inc(pool_d, 1)

                prepare(0, 0)
                difference(0, 0)
                difference(0, 1)
                with pool.Fori(0, HG_HEADS // 2) as i:
                    for w in range(2):
                        hd = 2 * i + w
                        for r in range(2, R):
                            difference(hd, r)
                        prepare(hd + 1, 1 - w)
                        difference(hd + 1, 0)
                        difference(hd + 1, 1)

            @block.tensor
            def _(pe):
                def feed(p, part):
                    pe.wait_ge(raw_in, 48 * p + 48)
                    for n in range(NG * part, NG * (part + 1)):
                        x, a, count = in_groups[n]
                        if n >= 4:
                            pe.wait_ge(in_read, p * NI + n - 3)
                        elif n == 0:
                            pe.wait_ge(ki_copied, p * 2 * NG)
                            pe.wait_ge(s_made, p * NS)
                        for c in range(count):
                            last = nc.tensor.transpose(in_ps[n % 4][:, c * P:(c + 1) * P], raw[:, x, a + c, :],
                                                       ident[:])
                        last.then_inc(in_turned, 1)

                def head(hd, w):
                    pe.wait_ge(in_read, (hd + 1) * NI)

                    def turn_keys(n):
                        d, a, count = ki_groups[n]
                        pe.wait_ge(w_ready, hd * R + d + 1)
                        if n >= 2:
                            pe.wait_ge(ki_copied, hd * 2 * NG + n - 1)
                        for c in range(count):
                            last = nc.tensor.transpose(tp[n % 2][:, c * P:(c + 1) * P],
                                                       W[:, d, 1, (a + c) * P:(a + c + 1) * P], ident[:])
                        last.then_inc(ki_turned, 1)

                    def pairs(n):
                        for g, (a, count) in enumerate(CHUNK_GROUPS):
                            if n >= 1:
                                pe.wait_ge(a_done, (hd * NL + n - 1) * NG + g + 1)
                            for c in range(count):
                                cols = slice((a + c) * P, (a + c + 1) * P)
                                slot = (n + 1) % WS
                                lhsT, rhs = (ksum[:, cols], qT[:, w, cols]) if n == 0 else \
                                    (W[:, slot, 1, cols], W[:, slot, 0, cols])
                                last = nc.tensor.matmul(l_ps[g][:, c * P:(c + 1) * P], lhsT, rhs,
                                                        start=True, stop=True)
                            last.then_inc(l_mm, 1)

                    for n in range(NG):
                        turn_keys(n)
                    pairs(0)
                    for n in range(NG, 2 * NG):
                        turn_keys(n)
                    pe.wait_ge(o_copied, hd * NG)
                    for n, (d, a, count) in enumerate(ki_groups):
                        pe.wait_ge(ki_copied, hd * 2 * NG + n + 1)
                        if n >= 2:
                            pe.wait_ge(s_made, hd * NS + made[n - 2])
                        for c in range(count):
                            last = nc.tensor.matmul(sp_ps[n % 2][:, c * P:(c + 1) * P], kiT[:, d, a + c, :],
                                                    v[:, a + c, bass.ds(hd * P, P)], start=True, stop=True)
                        last.then_inc(ds_mm, 1)
                    for n in range(1, NL):
                        pe.wait_ge(w_ready, hd * R + n + 2)
                        pairs(n)
                        if n <= 3:
                            feed(hd + 1, n - 1)
                    pe.wait_ge(a_done, (hd + 1) * NL * NG)
                    pe.wait_ge(s_made, (hd + 1) * NS)
                    pe.wait_ge(in_read, (hd + 2) * NI)
                    for g, (a, count) in enumerate(CHUNK_GROUPS):
                        if g >= 2:
                            pe.wait_ge(o_copied, hd * NG + g - 1)
                        for c in range(a, a + count):
                            to = sp_ps[g % 2][:, (c - a) * P:(c - a + 1) * P]
                            cols = slice(c * P, (c + 1) * P)
                            dirs = [d for d in range(2) if c not in (starts, ends)[d]]
                            last = nc.tensor.matmul(to, A[:, cols], v[:, c, bass.ds(hd * P, P)],
                                                    start=True, stop=not dirs)
                            for d in dirs:
                                last = nc.tensor.matmul(to, qi[:, d, cols], S[:, d, c, :], start=False,
                                                        stop=(d == dirs[-1]))
                        last.then_inc(o_mm, 1)

                for part in range(3):
                    feed(0, part)
                pe.wait_ge(v_in, 16)
                with pe.Fori(0, HG_HEADS // 2) as i:
                    for w in range(2):
                        head(2 * i + w, w)

            @block.scalar
            def _(act):
                act.wait_ge(chain, 1)
                nc.scalar.activation(lb_e[:], lb_e[:], ACT.Exp).then_inc(lb_ready, 1)

                def take_in(p, w, part):
                    for n in range(NG * part, NG * (part + 1)):
                        x, a, count = in_groups[n]
                        act.wait_ge(in_turned, p * NI + n + 1)
                        cols = slice(a * P, (a + count) * P)
                        to = qT[:, w, cols] if x == 0 else k[:, w, x - 1, cols]
                        nc.scalar.activation(to, in_ps[n % 4][:, 0:count * P], ACT.Copy).then_inc(in_read, 1)

                def gates(p, w):
                    act.wait_ge(in_read, (p + 1) * NI)
                    act.wait_ge(scanned, 2 * p)
                    for d in range(2):
                        nc.scalar.activation(f[:, d], k[:, w, d], ACT.Sigmoid)
                        nc.scalar.activation(k[:, w, d], k[:, w, d], ACT.Sigmoid, scale=-1.0).then_inc(z_done, 1)
                    act.wait_ge(q_done, p)
                    nc.scalar.activation(sgq[:], qT[:, w], ACT.Sigmoid).then_inc(sg_done, 1)

                def logarithms(p):
                    for d in range(2):
                        act.wait_ge(clamped, p * 2 + d + 1)
                        nc.scalar.activation(lf[:, d], lf[:, d], ACT.Ln)
                        nc.scalar.activation(f[:, d], f[:, d], ACT.Ln, scale=1.0 / LN_SPLIT).then_inc(ln_done, 1)

                def copy_keys(hd, d):
                    for n in range(d * NG, (d + 1) * NG):
                        _, a, count = ki_groups[n]
                        act.wait_ge(ki_turned, hd * 2 * NG + n + 1)
                        nc.scalar.activation(kiT[:, d, a:a + count, :],
                                             tp[n % 2][:, 0:count * P].rearrange("p (c t) -> p c t", t=P),
                                             ACT.Copy).then_inc(ki_copied, 1)

                def exp(hd, r):
                    act.wait_ge(pool_d, hd * R + r + 1)
                    z, y = (chunked(W[:, r % WS, x, :]) for x in range(2))
                    if r == 0:
                        nc.scalar.activation(z, e_with[:, 0], ACT.Exp)
                        nc.scalar.activation(y, y, ACT.Exp).then_inc(exp_done, 1)
                    elif r == 1:
                        nc.scalar.activation(y, e_to[:, 1], ACT.Exp)
                        nc.scalar.activation(z, z, ACT.Exp).then_inc(exp_done, 1)
                    else:
                        act.wait_ge(dve_d, hd * LEVELS + r - 1)
                        nc.scalar.activation(W[:, r % WS], W[:, r % WS], ACT.Exp).then_inc(exp_done, 1)

                def start(hd):
                    act.wait_ge(scanned, hd * 2 + 2)
                    nc.scalar.activation(decay[:], E[:, :, :, P], ACT.Exp).then_inc(dec_done, 1)
                    exp(hd, 0)
                    exp(hd, 1)

                def head(hd, w):
                    copy_keys(hd, 0)
                    for r in range(2, R):
                        exp(hd, r)
                        if r == 2:
                            copy_keys(hd, 1)
                        if r in (4, 5, 6):
                            take_in(hd + 1, 1 - w, r - 4)
                        if r == 6:
                            gates(hd + 1, 1 - w)
                    logarithms(hd + 1)
                    start(hd + 1)
                    act.wait_ge(stored, 16 * hd)
                    for g, (a, count) in enumerate(CHUNK_GROUPS):
                        act.wait_ge(o_mm, hd * NG + g + 1)
                        nc.scalar.activation(out[:, a:a + count, :],
                                             sp_ps[g % 2][:, 0:count * P].rearrange("p (c t) -> p c t", t=P),
                                             ACT.Copy).then_inc(o_copied, 1)

                for part in range(3):
                    take_in(0, 0, part)
                gates(0, 0)
                logarithms(0)
                start(0)
                with act.Fori(0, HG_HEADS // 2) as i:
                    for w in range(2):
                        head(2 * i + w, w)

            @block.vector
            def _(dve):
                step = Steps(SETUP)
                step.round(0)
                dve.wait_ge(lb_in, 32)
                nc.vector.tensor_tensor(lb_e[:], lb[:], lb[:], ALU.subtract).then_inc(chain, 1)
                step.next()
                dve.wait_ge(lb_ready, 1)
                nc.vector.reciprocal(lb_r[:], lb_e[:]).then_inc(chain, 1)
                dve.wait_ge(chain, step.next())
                nc.vector.tensor_tensor(lb_r[:], lb_e[:], lb_r[:], ALU.mult).then_inc(chain, 1)
                dve.wait_ge(chain, step.next())
                nc.vector.tensor_tensor(lb[:], lb_r[:], lb_r[:], ALU.subtract).then_inc(chain, 1)
                dve.wait_ge(chain, step.next())
                nc.vector.tensor_scalar(omlb[:], lb[:], -1.0, 1.0, ALU.mult, ALU.add).then_inc(chain, 1)
                step.next()
                dve.wait_ge(iota_done, 2)
                nc.vector.tensor_tensor(xor_i[:], cols_i[:], rows_i[:], ALU.bitwise_xor).then_inc(chain, 1)
                dve.wait_ge(chain, step.next())
                for n in range(LEVELS):
                    m = P >> (n + 1)
                    nc.vector.tensor_scalar(below[:], xor_i[:], 2.0 * m, None, ALU.is_lt).then_inc(chain, 1)
                    dve.wait_ge(chain, step.next())
                    nc.vector.scalar_tensor_tensor(mask[:, n, :], xor_i[:], float(m), below[:], ALU.is_ge, ALU.mult)\
                      .then_inc(chain, 1)
                    dve.wait_ge(chain, step.next())
                    if n < 4:
                        nc.vector.tensor_copy(diag[:, n, :], ident[:]).then_inc(chain, 1)
                    elif n < 6:
                        nc.vector.memset(E[:, n - 4, :, 0:1], 0.0).then_inc(chain, 1)
                    else:
                        nc.vector.memset(below[:, 0:1], 0.0).then_inc(chain, 1)
                    step.next()
                dve.wait_ge(chain, SETUP)

                def prepare(p, w):
                    count_of = Steps(PER)
                    count_of.base = SETUP + p * PER
                    for d in range(2):
                        dve.wait_ge(z_done, p * 2 + d + 1)
                        one_less, low = (x[:, d, bass.ds(p % HG_HEADS, 1)] for x in (omlb, lb))
                        nc.vector.tensor_scalar(k[:, w, d], k[:, w, d], one_less, None, ALU.mult).then_inc(chain, 1)
                        count_of.next()
                        nc.vector.tensor_scalar(f[:, d], f[:, d], one_less, low, ALU.mult, ALU.add).then_inc(chain, 1)
                        dve.wait_ge(chain, count_of.next())
                        nc.vector.tensor_scalar(lf[:, d], f[:, d], LN_SPLIT, None, ALU.max).then_inc(chain, 1)
                        dve.wait_ge(chain, count_of.next())
                        nc.vector.tensor_scalar(f[:, d], f[:, d], F_MIN, LN_SPLIT, ALU.max, ALU.min)\
                          .then_inc(clamped, 1)

                def run_sums(p):
                    for d in range(2):
                        dve.wait_ge(ln_done, p * 2 + d + 1)
                        for c in range(NT):
                            last = nc.vector.tensor_tensor_scan(E[:, d, c, 1:P + 1], lf[:, d, c * P:(c + 1) * P],
                                                                f[:, d, c * P:(c + 1) * P], 0.0, ALU.add, ALU.add)
                        last.then_inc(scanned, 1)

                def head(hd, w):
                    def differences(r):
                        if r >= 2:
                            wait_slot(dve, hd, r)
                            to, a, b = exponents(r)[3]
                            nc.vector.tensor_tensor(to, a, b, ALU.subtract).then_inc(dve_d, 1)

                    def weights(r):
                        dve.wait_ge(exp_done, hd * R + r + 1)
                        z, y = W[:, r % WS, 0], W[:, r % WS, 1]
                        if r >= 2:
                            nc.vector.tensor_tensor(z, z, qT[:, w], ALU.mult)
                        else:
                            nc.vector.tensor_tensor(y, y, k[:, w, r], ALU.mult).then_inc(w_ready, 1)
                            return
                        m = P >> (r - 1)
                        for side in range(2):
                            part = halves(chunked(y), m, side)
                            last = nc.vector.tensor_tensor(part, part, halves(chunked(k[:, w, side]), m, side),
                                                           ALU.mult)
                        last.then_inc(w_ready, 1)

                    def gather(n):
                        for g, (a, count) in enumerate(CHUNK_GROUPS):
                            cols, width = slice(a * P, (a + count) * P), count * P
                            if n == 0:
                                dve.wait_ge(l_mm, (hd * NL + n) * NG + g + 1)
                                nc.vector.tensor_tensor(A[:, cols], l_ps[g][:, 0:width],
                                                        diag[:, 0:count].rearrange("p c t -> p (c t)"), ALU.mult)\
                                  .then_inc(a_done, 1)
                            else:
                                products = held(dve, (hd * NL + n) * NG + g + 1)
                                before = held(dve, (hd * NL + n - 1) * NG + g + 1)
                                dve.wait_ge(chain, SETUP)
                                dve.wait_ge(l_mm, products)
                                dve.wait_ge(a_done, before)
                                nc.vector.copy_predicated(A[:, cols], mask[:, n - 1, 0:width], l_ps[g][:, 0:width])\
                                  .then_inc(a_done, 1)

                    def states():
                        dve.wait_ge(dec_done, hd + 1)
                        steps = 0
                        for n, (d, a, count) in enumerate(ki_groups):
                            dve.wait_ge(ds_mm, hd * 2 * NG + n + 1)
                            order = list(range(a, a + count))
                            for c in order if d == 0 else reversed(order):
                                to = c + 1 - 2 * d
                                if c in (ends, starts)[d]:
                                    continue
                                steps += 1
                                add = sp_ps[n % 2][:, (c - a) * P:(c - a + 1) * P]
                                if c in (starts, ends)[d]:
                                    nc.vector.tensor_copy(S[:, d, to, :], add).then_inc(s_made, 1)
                                else:
                                    nc.vector.scalar_tensor_tensor(S[:, d, to, :], S[:, d, c, :], decay[:, d, c:c + 1],
                                                                   add, ALU.mult, ALU.add).then_inc(s_made, 1)
                                dve.wait_ge(s_made, hd * NS + steps)

                    weights(0)
                    weights(1)
                    differences(2)
                    dve.wait_ge(q_done, hd + 1)
                    dve.wait_ge(o_mm, hd * NG)
                    for d in range(2):
                        nc.vector.tensor_tensor(qi[:, d], W[:, d, 0], qT[:, w], ALU.mult).then_inc(qi_done, 1)
                    gather(0)
                    for r in range(2, R):
                        if r + 1 < R:
                            differences(r + 1)
                        weights(r)
                        if r == 2:
                            states()
                        if r >= 3:
                            gather(r - 2)
                        if r == 7:
                            prepare(hd + 1, 1 - w)
                    run_sums(hd + 1)
                    gather(R - 2)

                prepare(0, 0)
                run_sums(0)
                with dve.Fori(0, HG_HEADS // 2) as i:
                    for w in range(2):
                        head(2 * i + w, w)


def stage_mix(nc, ident, h, aT, o, norm_g, w_na, w_hg, mix, wraw, w_out):
    KB = NAW // P
    with ExitStack() as ctx:
        s = Stage(nc, ctx, "mix")
        w_hi, w_lo = s.sb("w_hi", [P, 2, KB, D], F32R), s.sb("w_lo", [P, 2, KB, D], F32R)
        a_in, o_in, g_in = s.sb("a_in", [P, 2, KB, P]), s.sb("o_in", [P, 2, HGW]), s.sb("g_in", [P, 2, HGW])
        gates = s.sb("gates", [P, 2, 2, D])
        norm_all = s.sb("norm_all", [P, HGW])
        act_hi, act_lo = (s.sb(n, [P, 2, 2, KB, P], F32R) for n in ("act_hi", "act_lo"))
        sg, gg, sq, on, oh = (s.sb(n, [P, 2, HGW]) for n in ("sg", "gg", "sq", "on", "oh"))
        ss, rstd, mhalf = s.sb("ss", [P, 2, HG_HEADS]), s.sb("rstd", [P, 2, HG_HEADS]), s.sb("mhalf", [P, HG_HEADS])
        prod = s.sb("prod", [P, 2, 2, 2, 512])
        out = s.sb("out", [P, 2, D])
        tp = [s.ps(f"tp{u}", [P, 512]) for u in range(2)]
        acc = [[s.ps(f"acc{x}{b}", [P, 512]) for b in range(2)] for x in range(2)]
        w_hi_done, w_lo_done, norm_in, w_out_in = (s.sem(n) for n in ("w_hi_done", "w_lo_done", "norm_in", "w_out_in"))
        w_in = s.sems("w_in", 2)
        loaded, gates_in, stored = s.sems("loaded", 2), s.sems("gates_in", 2), s.sems("stored", 2)
        multiplied = s.sems("multiplied", 2)
        formed, used, gates_done = s.sems("formed", 2), s.sems("used", 2), s.sem("gates_done")
        (sg_done, a_hi, a_lo, gg_half, gg_done, half_made, squared, scaled, ss_done, var_done, rstd_done, oh_done,
         oh_turned, o_hi, acc_done, prod_done) = (s.sem(n) for n in (
             "sg_done", "a_hi", "a_lo", "gg_half", "gg_done", "half_made", "squared", "scaled", "ss_done",
             "var_done", "rstd_done", "oh_done", "oh_turned", "o_hi", "acc_done", "prod_done"))
        out_done = s.sems("out_done", 2)
        with nc.Block() as block:
            @block.sync
            def _(sp):
                for b, w in enumerate((w_na, w_hg)):
                    sp.dma_start(wraw[b][:], w.rearrange("(k p) n -> p k n", p=P)).then_inc(w_in[b], 16)
                sp.dma_start(norm_all[:], rows_of(norm_g, HGW)).then_inc(norm_in, 16)

                def load(t, u, r):
                    rows = bass.ds(t * P, P)
                    sp.wait_ge(formed[u], r)
                    sp.dma_start(a_in[:, u], aT[:, rows].rearrange("(k p) t -> p k t", p=P)).then_inc(loaded[u], 16)
                    sp.dma_start(o_in[:, u], o[rows, :]).then_inc(loaded[u], 16)
                    sp.dma_start(g_in[:, u], h[rows, COL_G:COL_G + HGW]).then_inc(loaded[u], 16)

                def load_gates(t, u, r):
                    sp.wait_ge(used[u], r)
                    sp.dma_start(gates[:, u].rearrange("p b n -> p (b n)"),
                                 h[bass.ds(t * P, P), COL_GATE:COL_GATE + 2 * D]).then_inc(gates_in[u], 16)

                in_steps(sp, [(0, load), (1, load_gates)])
                for n in range(2):
                    sp.wait_ge(w_lo_done, n + 1)
                    sp.dma_start(wraw[n][:], w_out[n * NAW:(n + 1) * NAW, :].rearrange("(k p) n -> p k n", p=P))\
                      .then_inc(w_out_in, 16)
                sp.wait_ge(w_out_in, 32)

            @block.scalar
            def _(act):
                for b in range(2):
                    act.wait_ge(w_in[b], 16)
                    nc.scalar.activation(w_hi[:, b], wraw[b][:], ACT.Copy).then_inc(w_hi_done, 1)

                def prepare(t, u, r):
                    act.wait_ge(loaded[u], 48 * r + 48)
                    act.wait_ge(formed[u], r)
                    nc.scalar.activation(sg[:, u], g_in[:, u], ACT.Sigmoid).then_inc(sg_done, 1)

                def form(t, u, r):
                    act.wait_ge(multiplied[u], r)
                    nc.scalar.activation(act_hi[:, u, 0], a_in[:, u], ACT.Copy).then_inc(a_hi, 1)
                    act.wait_ge(oh_turned, t + 1)
                    nc.scalar.activation(act_hi[:, u, 1], tp[u][:].rearrange("p (k c) -> p k c", k=KB), ACT.Copy)\
                      .then_inc(o_hi, 1)

                def open_gates(t, u, r):
                    act.wait_ge(gates_in[u], 16 * r + 16)
                    nc.scalar.activation(gates[:, u], gates[:, u], ACT.Sigmoid).then_inc(gates_done, 1)

                in_steps(act, [(0, prepare), (1, form), (2, open_gates)])

            @block.gpsimd
            def _(pool):
                nc.gpsimd.memset(mhalf[:], -0.5).then_inc(half_made, 1)
                pool.wait_ge(norm_in, 16)
                pool.wait_ge(half_made, 1)

                def prepare(t, u, r):
                    pool.wait_ge(sg_done, t + 1)
                    nc.gpsimd.tensor_tensor(gg[:, u], g_in[:, u], sg[:, u], ALU.mult).then_inc(gg_half, 1)
                    pool.wait_ge(gg_half, t + 1)
                    nc.gpsimd.tensor_tensor(gg[:, u], gg[:, u], norm_all[:], ALU.mult).then_inc(gg_done, 1)
                    count = held(pool, t + 1)
                    pool.wait_ge(half_made, 1)
                    pool.wait_ge(ss_done, count)
                    nc.gpsimd.tensor_scalar(ss[:, u], ss[:, u], 1.0 / P, RMS_EPS, ALU.mult, ALU.add)\
                      .then_inc(var_done, 1)
                    pool.wait_ge(var_done, t + 1)
                    nc.gpsimd.tensor_tensor(rstd[:, u], ss[:, u], mhalf[:], ALU.pow).then_inc(rstd_done, 1)

                def add(t, u, r):
                    pool.wait_ge(stored[u], 16 * r)
                    for x in range(2):
                        if x == 0:
                            pool.wait_ge(prod_done, t + 1)
                        else:
                            pool.wait_ge(used[u], r + 1)
                        last = nc.gpsimd.tensor_tensor(out[:, u, x * 512:(x + 1) * 512], prod[:, u, x, 0],
                                                       prod[:, u, x, 1], ALU.add)
                    last.then_inc(out_done[u], 1)
                    count = held(pool, r + 1)
                    pool.wait_ge(half_made, 1)
                    pool.wait_ge(out_done[u], count)
                    pool.dma_start(mix[bass.ds(t * P, P), :], out[:, u]).then_inc(stored[u], 16)

                in_steps(pool, [(0, prepare), (3, add)])
                for u in range(2):
                    pool.wait_ge(stored[u], 16 * (NT // 2))

            @block.vector
            def _(dve):
                for b in range(2):
                    dve.wait_ge(w_hi_done, b + 1)
                    nc.vector.tensor_tensor(w_lo[:, b], wraw[b][:], w_hi[:, b].bitcast(F32), ALU.subtract)\
                      .then_inc(w_lo_done, 1)

                def prepare(t, u, r):
                    dve.wait_ge(loaded[u], 48 * r + 48)
                    nc.vector.tensor_tensor(sq[:, u], o_in[:, u], o_in[:, u], ALU.mult).then_inc(squared, 1)
                    dve.wait_ge(squared, t + 1)
                    nc.vector.tensor_reduce(ss[:, u], sq[:, u].rearrange("p (h c) -> p h c", c=P), AX.X, ALU.add)\
                      .then_inc(ss_done, 1)

                def form(t, u, r):
                    dve.wait_ge(a_hi, t + 1)
                    nc.vector.tensor_tensor(act_lo[:, u, 0], a_in[:, u], act_hi[:, u, 0].bitcast(F32), ALU.subtract)\
                      .then_inc(a_lo, 1)
                    dve.wait_ge(rstd_done, t + 1)
                    nc.vector.tensor_tensor(on[:, u].rearrange("p (h c) -> p h c", c=P),
                                            o_in[:, u].rearrange("p (h c) -> p h c", c=P),
                                            rstd[:, u].unsqueeze(2).to_broadcast([P, HG_HEADS, P]), ALU.mult)\
                      .then_inc(scaled, 1)
                    dve.wait_ge(scaled, t + 1)
                    dve.wait_ge(gg_done, t + 1)
                    nc.vector.tensor_tensor(oh[:, u], on[:, u], gg[:, u], ALU.mult).then_inc(oh_done, 1)

                def split(t, u, r):
                    dve.wait_ge(o_hi, t + 1)
                    nc.vector.tensor_tensor(act_lo[:, u, 1], tp[u][:].rearrange("p (k c) -> p k c", k=KB),
                                            act_hi[:, u, 1].bitcast(F32), ALU.subtract)\
                      .then_inc(formed[u], 1)

                def weigh(t, u, r):
                    dve.wait_ge(gates_done, t + 1)
                    dve.wait_ge(out_done[u], r)
                    for x in range(2):
                        if x == 0:
                            dve.wait_ge(acc_done, t + 1)
                        else:
                            dve.wait_ge(multiplied[u], r + 1)
                        for b in range(2):
                            last = nc.vector.tensor_tensor(prod[:, u, x, b], acc[x][b][:],
                                                           gates[:, u, b, x * 512:(x + 1) * 512], ALU.mult)
                        last.then_inc(prod_done if x == 0 else used[u], 1)

                in_steps(dve, [(0, prepare), (1, form), (3, weigh), (1, split)])

            @block.tensor
            def _(pe):
                def turn(t, u, r):
                    pe.wait_ge(oh_done, t + 1)
                    for k in range(KB):
                        last = nc.tensor.transpose(tp[u][:, k * P:(k + 1) * P], oh[:, u, k * P:(k + 1) * P], ident[:])
                    last.then_inc(oh_turned, 1)

                def product(t, u, r):
                    pe.wait_ge(w_lo_done, 2)
                    pe.wait_ge(a_lo, t + 1)
                    pe.wait_ge(formed[u], r + 1)
                    for x in range(2):
                        cols = slice(x * 512, (x + 1) * 512)
                        if x == 0:
                            pe.wait_ge(prod_done, t)
                        else:
                            pe.wait_ge(used[1 - u], r + u)
                        for b in range(2):
                            for k in range(KB):
                                hi, lo = act_hi[:, u, b, k, :], act_lo[:, u, b, k, :]
                                nc.tensor.matmul(acc[x][b][:], hi, w_hi[:, b, k, cols], start=(k == 0), stop=False)
                                nc.tensor.matmul(acc[x][b][:], hi, w_lo[:, b, k, cols], start=False, stop=False)
                                last = nc.tensor.matmul(acc[x][b][:], lo, w_hi[:, b, k, cols], start=False,
                                                        stop=(k == KB - 1))
                        last.then_inc(acc_done if x == 0 else multiplied[u], 1)

                in_steps(pe, [(1, turn), (2, product)])


def stage_out(nc, ident, mix, xln, wraw, g, b, w_router, x1, y, affT):
    with ExitStack() as ctx:
        s = Stage(nc, ctx, "out")
        w_hi, w_lo = s.sb("w_hi", [P, KD, D], F32R), s.sb("w_lo", [P, KD, D], F32R)
        wr = s.sb("wr", [P, KD, NE])
        g_all, b_all = s.sb("g_all", [P, D]), s.sb("b_all", [P, D])
        mix_in, x_in = s.sb("mix_in", [P, 2, D]), s.sb("x_in", [P, 2, D])
        m_hi, m_lo = s.sb("m_hi", [P, 2, KD, P], F32R), s.sb("m_lo", [P, 2, KD, P], F32R)
        x1_sb, y_sb = s.sb("x1_sb", [P, 2, D]), s.sb("y_sb", [P, 2, D])
        x1T = s.sb("x1T", [P, KD, P])
        stats, mv, veps, rstd, mhalf = (s.sb(n, sh) for n, sh in (
            ("stats", [P, 2, 6]), ("mv", [P, 2]), ("veps", [P, 1]), ("rstd", [P, 1]), ("mhalf", [P, 1])))
        nmax, total, inv, aff = (s.sb(n, sh) for n, sh in (
            ("nmax", [P, 1]), ("total", [P, 1]), ("inv", [P, 1]), ("aff", [P, NE])))
        tp, tx = s.ps("tp", [P, D]), s.ps("tx", [P, D])
        acc = [s.ps(f"acc{x}", [P, 512]) for x in range(2)]
        lg, at = s.ps("lg", [P, NE]), s.ps("at", [NE, P])
        w_hi_done, w_lo_done, small_in = (s.sem(n) for n in ("w_hi_done", "w_lo_done", "small_in"))
        x_read, x_loaded, m_turned, x1_turned = (s.sems(n, 2) for n in ("x_read", "x_loaded", "m_turned", "x1_turned"))
        summed = s.sems("summed", 2)
        loaded, stored_x, stored_y = s.sems("loaded", 2), s.sems("stored_x", 2), s.sems("stored_y", 2)
        (m_hi_done, m_lo_done, acc_done, chain, var_ready, var_eps, rstd_ready, centred, x1_done,
         y_done, x1_copied, lg_done, maxed, exp_done, inverted, aff_done, aff_turned, aff_copied,
         half_made) = (s.sem(n) for n in (
             "m_hi_done", "m_lo_done", "acc_done", "chain", "var_ready", "var_eps",
             "rstd_ready", "centred", "x1_done", "y_done", "x1_copied", "lg_done", "maxed", "exp_done",
             "inverted", "aff_done", "aff_turned", "aff_copied", "half_made"))
        with nc.Block() as block:
            @block.sync
            def _(sp):
                sp.dma_start(wr[:], w_router.rearrange("(k p) e -> p k e", p=P)).then_inc(small_in, 16)
                sp.dma_start(g_all[:], rows_of(g, D)).then_inc(small_in, 16)
                sp.dma_start(b_all[:], rows_of(b, D)).then_inc(small_in, 16)

                def load(t, u, r):
                    sp.wait_ge(m_turned[u], r)
                    sp.dma_start(mix_in[:, u], mix[bass.ds(t * P, P), :]).then_inc(loaded[u], 16)

                def load_x(t, u, r):
                    sp.wait_ge(x_read[u], r)
                    sp.dma_start(x_in[:, u], xln[bass.ds(t * P, P), :]).then_inc(x_loaded[u], 16)

                in_steps(sp, [(0, load), (1, load_x)])

            @block.scalar
            def _(act):
                for v in range(2):
                    nc.scalar.activation(w_hi[:, 4 * v:4 * v + 4], wraw[v][:], ACT.Copy).then_inc(w_hi_done, 1)

                def split(t, u, r):
                    act.wait_ge(m_turned[u], r + 1)
                    for x in range(2):
                        last = nc.scalar.activation(m_hi[:, u, 4 * x:4 * x + 4],
                                                    tp[:, x * 512:(x + 1) * 512].rearrange("p (k c) -> p k c", k=4),
                                                    ACT.Copy)
                    last.then_inc(m_hi_done, 1)

                def scale(t, u, r):
                    act.wait_ge(x1_done, t + 1)
                    act.wait_ge(stored_y[u], 16 * r)
                    nc.scalar.activation(y_sb[:, u], x1_sb[:, u], ACT.Copy, scale=ALPHA).then_inc(y_done, 1)

                def copy_x1(t, u, r):
                    act.wait_ge(x1_turned[u], r + 1)
                    act.wait_ge(lg_done, t)
                    for x in range(2):
                        last = nc.scalar.activation(x1T[:, 4 * x:4 * x + 4],
                                                    tx[:, x * 512:(x + 1) * 512].rearrange("p (k c) -> p k c", k=4),
                                                    ACT.Copy)
                    last.then_inc(x1_copied, 1)

                def exp(t, u, r):
                    act.wait_ge(maxed, t + 1)
                    act.wait_ge(aff_turned, t)
                    nc.scalar.activation(aff[:], lg[:], ACT.Exp, bias=nmax[:], accum_out=total[:]).then_inc(exp_done, 1)

                in_steps(act, [(0, split), (3, copy_x1), (2, scale), (4, exp)])

            @block.gpsimd
            def _(pool):
                nc.gpsimd.memset(mhalf[:], -0.5).then_inc(half_made, 1)
                pool.wait_ge(half_made, 1)

                def norm(t, u, r):
                    count = held(pool, t + 1)
                    pool.wait_ge(half_made, 1)
                    pool.wait_ge(var_ready, count)
                    nc.gpsimd.tensor_scalar(veps[:], mv[:, 1:2], LN_EPS, None, ALU.add).then_inc(var_eps, 1)
                    pool.wait_ge(var_eps, t + 1)
                    nc.gpsimd.tensor_tensor(rstd[:], veps[:], mhalf[:], ALU.pow).then_inc(rstd_ready, 1)
                    rows = bass.ds(t * P, P)
                    pool.wait_ge(x1_done, t + 1)
                    pool.dma_start(x1[rows, :], x1_sb[:, u]).then_inc(stored_x[u], 16)
                    count = held(pool, t + 1)
                    pool.wait_ge(half_made, 1)
                    pool.wait_ge(y_done, count)
                    pool.dma_start(y[rows, :], y_sb[:, u]).then_inc(stored_y[u], 16)

                in_steps(pool, [(2, norm)])
                for u in range(2):
                    pool.wait_ge(stored_x[u], 16 * (NT // 2))
                    pool.wait_ge(stored_y[u], 16 * (NT // 2))

            @block.vector
            def _(dve):
                for v in range(2):
                    dve.wait_ge(w_hi_done, v + 1)
                    nc.vector.tensor_tensor(w_lo[:, 4 * v:4 * v + 4], wraw[v][:],
                                            w_hi[:, 4 * v:4 * v + 4].bitcast(F32), ALU.subtract)\
                      .then_inc(w_lo_done, 1)
                dve.wait_ge(small_in, 48)

                def split(t, u, r):
                    dve.wait_ge(m_hi_done, t + 1)
                    for x in range(2):
                        last = nc.vector.tensor_tensor(m_lo[:, u, 4 * x:4 * x + 4],
                                                       tp[:, x * 512:(x + 1) * 512].rearrange("p (k c) -> p k c", k=4),
                                                       m_hi[:, u, 4 * x:4 * x + 4].bitcast(F32), ALU.subtract)
                    last.then_inc(m_lo_done, 1)

                def add_up(t, u, r):
                    dve.wait_ge(x_loaded[u], 16 * r + 16)
                    for x in range(2):
                        cols = slice(x * 512, (x + 1) * 512)
                        dve.wait_ge(acc_done, 2 * t + x + 1)
                        nc.vector.scalar_tensor_tensor(x_in[:, u, cols], x_in[:, u, cols], ALPHA, acc[x][:],
                                                       ALU.mult, ALU.add).then_inc(summed[x], 1)
                    for x in range(2):
                        dve.wait_ge(summed[x], t + 1)
                        nc.vector.bn_stats(stats[:, x, :], x_in[:, u, x * 512:(x + 1) * 512]).then_inc(chain, 1)
                    count = held(dve, 3 * t + 2)
                    dve.wait_ge(small_in, 48)
                    dve.wait_ge(chain, count)
                    nc.vector.bn_aggr(mv[:], stats[:]).then_inc(var_ready, 1)

                def centre(t, u, r):
                    dve.wait_ge(stored_x[u], 16 * r)
                    dve.wait_ge(stored_y[u], 16 * r)
                    dve.wait_ge(x1_turned[u], r)
                    dve.wait_ge(var_ready, t + 1)
                    dve.wait_ge(rstd_ready, t + 1)
                    nc.vector.tensor_scalar(x1_sb[:, u], x_in[:, u], mv[:, 0:1], rstd[:], ALU.subtract, ALU.mult)\
                      .then_inc(x_read[u], 1)
                    dve.wait_ge(x_read[u], r + 1)
                    nc.vector.tensor_tensor(x1_sb[:, u], x1_sb[:, u], g_all[:], ALU.mult).then_inc(chain, 1)
                    dve.wait_ge(chain, 3 * t + 3)
                    nc.vector.tensor_tensor(x1_sb[:, u], x1_sb[:, u], b_all[:], ALU.add).then_inc(x1_done, 1)

                def find_max(t, u, r):
                    dve.wait_ge(lg_done, t + 1)
                    nc.vector.tensor_reduce(nmax[:], lg[:], AX.X, ALU.max, negate=True).then_inc(maxed, 1)

                def normalise(t, u, r):
                    dve.wait_ge(exp_done, t + 1)
                    nc.vector.reciprocal(inv[:], total[:]).then_inc(inverted, 1)
                    dve.wait_ge(inverted, t + 1)
                    nc.vector.tensor_scalar(aff[:], aff[:], inv[:], None, ALU.mult).then_inc(aff_done, 1)

                def keep(t, u, r):
                    dve.wait_ge(aff_turned, t + 1)
                    nc.vector.tensor_copy(affT[:, bass.ds(t * P, P)], at[:]).then_inc(aff_copied, 1)

                in_steps(dve, [(4, find_max), (2, add_up), (0, split), (2, centre), (4, normalise), (5, keep)])

            @block.tensor
            def _(pe):
                def turn(t, u, r):
                    pe.wait_ge(loaded[u], 16 * r + 16)
                    pe.wait_ge(m_lo_done, t)
                    for k in range(KD):
                        last = nc.tensor.transpose(tp[:, k * P:(k + 1) * P], mix_in[:, u, k * P:(k + 1) * P], ident[:])
                    last.then_inc(m_turned[u], 1)

                def product(t, u, r):
                    pe.wait_ge(w_lo_done, 2)
                    pe.wait_ge(m_lo_done, t + 1)
                    for x in range(2):
                        cols = slice(x * 512, (x + 1) * 512)
                        pe.wait_ge(summed[x], t)
                        for k in range(KD):
                            hi, lo = m_hi[:, u, k, :], m_lo[:, u, k, :]
                            nc.tensor.matmul(acc[x][:], hi, w_hi[:, k, cols], start=(k == 0), stop=False)
                            nc.tensor.matmul(acc[x][:], hi, w_lo[:, k, cols], start=False, stop=False)
                            last = nc.tensor.matmul(acc[x][:], lo, w_hi[:, k, cols], start=False, stop=(k == KD - 1))
                        last.then_inc(acc_done, 1)

                def turn_x1(t, u, r):
                    pe.wait_ge(x1_done, t + 1)
                    pe.wait_ge(x1_copied, t)
                    for k in range(KD):
                        last = nc.tensor.transpose(tx[:, k * P:(k + 1) * P], x1_sb[:, u, k * P:(k + 1) * P], ident[:])
                    last.then_inc(x1_turned[u], 1)

                def logits(t, u, r):
                    pe.wait_ge(small_in, 48)
                    pe.wait_ge(x1_copied, t + 1)
                    pe.wait_ge(exp_done, t)
                    for k in range(KD):
                        last = nc.tensor.matmul(lg[:], x1T[:, k, :], wr[:, k, :], start=(k == 0), stop=(k == KD - 1))
                    last.then_inc(lg_done, 1)

                def turn_aff(t, u, r):
                    pe.wait_ge(aff_done, t + 1)
                    pe.wait_ge(aff_copied, t)
                    nc.tensor.transpose(at[:], aff[:], ident[:]).then_inc(aff_turned, 1)

                in_steps(pe, [(5, turn_aff), (0, turn), (1, product), (2, turn_x1), (3, logits)])


RING = 6
SLICES = 4


def load_piece(sp, ring, w_ready, w_gate, w_up, w_down, e, n):
    if n < 2 * SLICES:
        w, q = (w_gate, w_up)[n % 2], n // 2
        src = w[bass.ds(e * D, D), q * 512:(q + 1) * 512]
    else:
        q = n - 2 * SLICES
        src = w_down[bass.ds(e * FF, FF), q * 256:(q + 1) * 256]
    to = ring[:, n % RING, :].rearrange("p (k n) -> p k n", n=src.shape[1])
    sp.dma_start(to, src.rearrange("(k p) n -> p k n", p=P)).then_inc(w_ready[n % RING], 16)


def stage_choose(nc, ident, affT, gates, picks, load_first_pieces):
    with ExitStack() as ctx:
        s = Stage(nc, ctx, "choose")
        best, at, at_f = s.sb("best", [NE, TOK]), s.sb("at", [NE, TOK], U32), s.sb("at_f", [NE, TOK])
        tp = s.ps("tp", [P, 2, 2, NE])
        cleared, chain, found, turned, made = (s.sem(n) for n in ("cleared", "chain", "found", "turned", "made"))
        first_slot = (0, CAPS[0])
        with nc.Block() as block:
            @block.sync
            def _(sp):
                load_first_pieces(sp)

            @block.gpsimd
            def _(pool):
                for n in range(2):
                    nc.gpsimd.memset(picks[n][:], 0).then_inc(cleared, 1)

            @block.vector
            def _(dve):
                steps = 0
                for n, (start, count) in enumerate(SEQS):
                    row = affT[:, start:start + count]
                    for c in range(first_slot[n], first_slot[n] + CAPS[n], 8):
                        for op in range(3):
                            if steps:
                                dve.wait_ge(chain, steps)
                            eight = best[:, c:c + 8]
                            if op == 0:
                                ins = nc.vector.max(eight, row)
                            elif op == 1:
                                ins = nc.vector.max_index(at[:, c:c + 8], eight, row)
                            else:
                                ins = nc.vector.match_replace(out=row, in_to_replace=eight, in_values=row,
                                                              imm_value=-1.0)
                            ins.then_inc(chain, 1)
                            steps += 1
                dve.wait_ge(chain, steps)
                for n, (start, _) in enumerate(SEQS):
                    cols = slice(first_slot[n], first_slot[n] + CAPS[n])
                    nc.vector.tensor_scalar(at_f[:, cols], at[:, cols], float(start), None, ALU.add).then_inc(found, 1)
                dve.wait_ge(turned, 1)
                dve.wait_ge(cleared, 2)
                for n in range(2):
                    nc.vector.tensor_copy(gates[n][:], tp[0:CAPS[n], n, 0, :]).then_inc(made, 1)
                    nc.vector.tensor_copy(picks[n][:, 0:NE], tp[0:CAPS[n], n, 1, :]).then_inc(made, 1)
                dve.wait_ge(made, 4)

            @block.tensor
            def _(pe):
                pe.wait_ge(found, 2)
                for n in range(2):
                    cols = slice(first_slot[n], first_slot[n] + CAPS[n])
                    nc.tensor.transpose(tp[0:CAPS[n], n, 0, :], best[:, cols], ident[0:NE, 0:NE])
                    last = nc.tensor.transpose(tp[0:CAPS[n], n, 1, :], at_f[:, cols], ident[0:NE, 0:NE])
                last.then_inc(turned, 1)


def stage_experts(nc, ident, x1, w_gate, w_up, w_down, gates, picks, y, ring, w_ready):
    UNITS = NFT // 2
    CP, CS = CAPS
    with ExitStack() as ctx:
        s = Stage(nc, ctx, "moe")
        rows_s, rows_p = s.sb("rows_s", [CS, D]), s.sb("rows_p", [CP, D])
        xT = s.sb("xT", [P, 2, KD, TOK])
        sil, hdn = s.sb("sil", [P, 2, 2, TOK]), s.sb("hdn", [P, NFT, TOK])
        outT = s.sb("outT", [P, KD, TOK])
        out_s, out_p = s.sb("out_s", [CS, D]), s.sb("out_p", [CP, D])
        at_in = [s.sb(f"at_in{n}", [CAPS[n], 1], U32) for n in range(2)]
        at_out = [s.sb(f"at_out{n}", [CAPS[n], 1], U32) for n in range(2)]
        gate_ps = [s.ps(f"gate{b}", [P, 2, TOK]) for b in range(2)]
        up_ps = [s.ps(f"up{b}", [P, 2, TOK]) for b in range(2)]
        down_ps = [s.ps(f"down{b}", [P, 2, TOK]) for b in range(2)]
        turn_ps = [s.ps(f"turn{b}", [P, 512]) for b in range(2)]
        gate_mm, up_mm, down_mm = s.sems("gate_mm", 2), s.sems("up_mm", 2), s.sems("down_mm", SLICES)
        silu_done, hdn_made, down_copied = s.sems("silu_done", 2), s.sems("hdn_made", 2), s.sems("down_copied", 2)
        gathered, in_turned, in_read = s.sem("gathered"), s.sem("in_turned"), s.sem("in_read")
        out_turned, out_read, added = s.sem("out_turned"), s.sem("out_read"), s.sem("added")
        at_ready = s.sem("at_ready")

        def fresh_piece(e, n):
            if n in (0, 1):
                return (gate_mm, up_mm)[n][1], SLICES * e
            if n < RING:
                return down_mm[n - 2], e
            return (gate_mm, up_mm)[n % 2][1], SLICES * e + (n - RING) // 2 + 1

        with nc.Block() as block:
            @block.sync
            def _(sp):
                for n in range(RING, 3 * SLICES):
                    sp.wait_ge(*fresh_piece(0, n))
                    load_piece(sp, ring, w_ready, w_gate, w_up, w_down, 0, n)
                with sp.Fori(1, NE) as e:
                    for n in range(3 * SLICES):
                        sp.wait_ge(*fresh_piece(e, n))
                        load_piece(sp, ring, w_ready, w_gate, w_up, w_down, e, n)

            @block.gpsimd
            def _(pool):
                def gather(e, lists):
                    for n in range(2):
                        nc.gpsimd.tensor_copy(at_in[n][:], picks[n][:, bass.ds(e, 1)]).then_inc(at_ready, 1)
                    count = held(pool, lists)
                    pool.wait_ge(at_ready, 2)
                    pool.wait_ge(at_ready, count)
                    for n, to in enumerate((rows_p, rows_s)):
                        pool.indirect_dma_start(to[:], None, x1, bass.IndirectOffsetOnAxis(at_in[n][:], 0))\
                            .then_inc(gathered, 16)

                gather(0, 2)
                with pool.Fori(0, NE) as e:
                    pool.wait_ge(in_turned, 3 * e + 3)
                    gather(e + 1, 4 * e + 4)
                    pool.wait_ge(added, 32 * e)
                    for n in range(2):
                        nc.gpsimd.tensor_copy(at_out[n][:], picks[n][:, bass.ds(e, 1)]).then_inc(at_ready, 1)
                    lists, rows = held(pool, 4 * e + 6), held(pool, 4 * e + 4)
                    pool.wait_ge(gathered, 32)
                    pool.wait_ge(at_ready, lists)
                    pool.wait_ge(out_read, rows)
                    for n, src in enumerate((out_p, out_s)):
                        pool.indirect_dma_start(y, bass.IndirectOffsetOnAxis(at_out[n][:], 0), src[:], None,
                                                compute_op=ALU.add).then_inc(added, 16)
                pool.wait_ge(added, 32 * NE)
                pool.wait_ge(gathered, 32 * (NE + 1))

            @block.tensor
            def _(pe):
                def turn_in(e, parts):
                    for j in parts:
                        if j == 0:
                            pe.wait_ge(gathered, 32 * e + 32)
                        if j == 2:
                            read = held(pe, 3 * e + 1)
                            pe.wait_ge(gathered, 32)
                            pe.wait_ge(in_read, read)
                            for k in range(KD):
                                last = nc.tensor.transpose(turn_ps[0][:, k * CP:(k + 1) * CP],
                                                           rows_p[:, k * P:(k + 1) * P], ident[0:CP, 0:CP])
                        else:
                            for k in range(4):
                                last = nc.tensor.transpose(turn_ps[j][:, k * P:(k + 1) * P],
                                                           rows_s[:, (4 * j + k) * P:(4 * j + k + 1) * P], ident[:])
                        last.then_inc(in_turned, 1)

                def turn_out(e, half):
                    for b in range(2):
                        pe.wait_ge(down_copied[b], 2 * e + half + 1)
                    for j in (2 * half, 2 * half + 1):
                        if half == 0:
                            pe.wait_ge(in_read, 3 * e + 5 + j)
                        else:
                            pe.wait_ge(out_read, 4 * e + j - 1)
                        part, b = (slice(0, CS), slice(CS, TOK))[j % 2], 1 - j % 2
                        for k in range(4):
                            last = nc.tensor.transpose(turn_ps[b][0:part.stop - part.start, k * P:(k + 1) * P],
                                                       outT[:, 4 * half + k, part], ident[:])
                        last.then_inc(out_turned, 1)

                def expert(e, w):
                    pe.wait_ge(in_read, 3 * e + 3)
                    for n in range(UNITS):
                        q, b = n // 2, n % 2
                        for m, ps, free, done in ((0, gate_ps, silu_done, gate_mm), (1, up_ps, hdn_made, up_mm)):
                            piece = 2 * q + m
                            pe.wait_ge(w_ready[piece % RING], 32 * e + 16 * (piece // RING) + 16)
                            pe.wait_ge(free[b], 4 * e + q)
                            weights = ring[:, piece % RING, :].rearrange("p (k n) -> p k n", n=512)
                            for f in range(2):
                                c = (2 * b + f) * P
                                for k in range(KD):
                                    last = nc.tensor.matmul(ps[b][:, f, :], weights[:, k, c:c + P], xT[:, w, k, :],
                                                            start=(k == 0), stop=(k == KD - 1))
                            last.then_inc(done[b], 1)
                        if n == 3:
                            pe.wait_ge(out_read, 4 * e)
                            turn_in(e + 1, (0, 1))
                        if n == 4:
                            turn_in(e + 1, (2,))
                    pe.wait_ge(hdn_made[0], 4 * e + 4)
                    pe.wait_ge(hdn_made[1], 4 * e + 3)
                    for q in range(SLICES):
                        b, piece = q % 2, 2 * SLICES + q
                        pe.wait_ge(w_ready[piece % RING], 32 * e + 32)
                        pe.wait_ge(down_copied[b], 2 * e + q // 2)
                        weights = ring[:, piece % RING, :].rearrange("p (k n) -> p k n", n=256)
                        for d in range(2):
                            for f in range(NFT):
                                if q == 0 and d == 0 and f == NFT - 2:
                                    pe.wait_ge(hdn_made[1], 4 * e + 4)
                                last = nc.tensor.matmul(down_ps[b][:, d, :], weights[:, f, d * P:(d + 1) * P],
                                                        hdn[:, f, :], start=(f == 0), stop=(f == NFT - 1))
                        last.then_inc(down_mm[q], 1)
                        if q >= 2:
                            turn_out(e, q - 2)

                turn_in(0, range(3))
                with pe.Fori(0, NE // 2) as i:
                    for w in range(2):
                        expert(2 * i + w, w)

            @block.scalar
            def _(act):
                with act.Fori(0, NE) as e:
                    for n in range(UNITS):
                        q, b = n // 2, n % 2
                        act.wait_ge(gate_mm[b], 4 * e + q + 1)
                        act.wait_ge(hdn_made[b], 4 * e + q)
                        nc.scalar.activation(sil[:, b], gate_ps[b][:], ACT.Silu).then_inc(silu_done[b], 1)
                    for q in range(SLICES):
                        act.wait_ge(down_mm[q], e + 1)
                        nc.scalar.activation(outT[:, 2 * q:2 * q + 2, :], down_ps[q % 2][:], ACT.Copy)\
                          .then_inc(down_copied[q % 2], 1)

            @block.vector
            def _(dve):
                def copy_in(e, w, parts):
                    for j in parts:
                        dve.wait_ge(in_turned, 3 * e + j + 1)
                        if j == 2:
                            to, ps = xT[:, w, :, CS:TOK], turn_ps[0][:, 0:KD * CP].rearrange("p (k c) -> p k c", k=KD)
                        else:
                            to, ps = xT[:, w, 4 * j:4 * j + 4, 0:CS], turn_ps[j][:].rearrange("p (k c) -> p k c", k=4)
                        nc.vector.tensor_copy(to, ps).then_inc(in_read, 1)

                def expert(e, w):
                    for n in range(UNITS):
                        q, b = n // 2, n % 2
                        dve.wait_ge(silu_done[b], 4 * e + q + 1)
                        dve.wait_ge(up_mm[b], 4 * e + q + 1)
                        if n == 0:
                            dve.wait_ge(down_mm[SLICES - 1], e)
                        nc.vector.tensor_tensor(hdn[:, 2 * n:2 * n + 2, :], sil[:, b], up_ps[b][:], ALU.mult)\
                          .then_inc(hdn_made[b], 1)
                        if n == 3:
                            copy_in(e + 1, 1 - w, (0, 1))
                        if n == 4:
                            copy_in(e + 1, 1 - w, (2,))
                    dve.wait_ge(added, 32 * e)
                    for j in range(4):
                        dve.wait_ge(out_turned, 4 * e + j + 1)
                        x, half = 1 - j % 2, slice(j // 2 * 512, (j // 2 + 1) * 512)
                        to = (out_p, out_s)[x]
                        nc.vector.tensor_scalar(to[:, half], turn_ps[x][0:CAPS[x], :], gates[x][:, bass.ds(e, 1)], None,
                                                ALU.mult).then_inc(out_read, 1)

                copy_in(0, 0, range(3))
                with dve.Fori(0, NE // 2) as i:
                    for w in range(2):
                        expert(2 * i + w, w)


def stage_norm_out(nc, y, g, b, out):
    with ExitStack() as ctx:
        s = Stage(nc, ctx, "ln2")
        x_in, centred, x_out = (s.sb(n, [P, 2, D]) for n in ("x_in", "centred", "x_out"))
        g_all, b_all = s.sb("g_all", [P, D]), s.sb("b_all", [P, D])
        stats, mv, veps, rstd, mhalf = (s.sb(n, sh) for n, sh in (
            ("stats", [P, 2, 2, 6]), ("mv", [P, 2, 2]), ("veps", [P, 2]), ("rstd", [P, 2]), ("mhalf", [P, 1])))
        consts_in, half_made, var_eps, chain, var_ready = (s.sem(n) for n in (
            "consts_in", "half_made", "var_eps", "chain", "var_ready"))
        rstd_ready, x_ready, x_read, scaled, out_ready, stored = (s.sems(n, 2) for n in (
            "rstd_ready", "x_ready", "x_read", "scaled", "out_ready", "stored"))
        with nc.Block() as block:
            @block.sync
            def _(sp):
                sp.dma_start(g_all[:], rows_of(g, D)).then_inc(consts_in, 16)
                sp.dma_start(b_all[:], rows_of(b, D)).then_inc(consts_in, 16)

                def load(t, u, r):
                    sp.wait_ge(x_read[u], r)
                    sp.dma_start(x_in[:, u], y[bass.ds(t * P, P), :]).then_inc(x_ready[u], 16)

                in_steps(sp, [(0, load)])

            @block.vector
            def _(dve):
                def measure(t, u, r):
                    dve.wait_ge(x_ready[u], 16 * r + 16)
                    for x in range(2):
                        nc.vector.bn_stats(stats[:, u, x, :], x_in[:, u, x * 512:(x + 1) * 512]).then_inc(chain, 1)
                    count = held(dve, 2 * t + 2)
                    dve.wait_ge(consts_in, 32)
                    dve.wait_ge(chain, count)
                    nc.vector.bn_aggr(mv[:, u], stats[:, u]).then_inc(var_ready, 1)

                def shift(t, u, r):
                    dve.wait_ge(scaled[u], r + 1)
                    nc.vector.tensor_tensor(x_out[:, u], x_out[:, u], b_all[:], ALU.add).then_inc(out_ready[u], 1)

                def centre(t, u, r):
                    dve.wait_ge(scaled[u], r)
                    dve.wait_ge(var_ready, t + 1)
                    dve.wait_ge(rstd_ready[u], r + 1)
                    nc.vector.tensor_scalar(centred[:, u], x_in[:, u], mv[:, u, 0:1], rstd[:, u:u + 1], ALU.subtract,
                                            ALU.mult).then_inc(x_read[u], 1)

                dve.wait_ge(consts_in, 32)
                in_steps(dve, [(1, centre), (0, measure), (2, shift)])

            @block.gpsimd
            def _(pool):
                nc.gpsimd.memset(mhalf[:], -0.5).then_inc(half_made, 1)
                pool.wait_ge(half_made, 1)
                pool.wait_ge(consts_in, 32)

                def invert(t, u, r):
                    count = held(pool, t + 1)
                    pool.wait_ge(half_made, 1)
                    pool.wait_ge(var_ready, count)
                    nc.gpsimd.tensor_scalar(veps[:, u:u + 1], mv[:, u, 1:2], LN_EPS, None, ALU.add).then_inc(var_eps, 1)
                    pool.wait_ge(var_eps, t + 1)
                    nc.gpsimd.tensor_tensor(rstd[:, u:u + 1], veps[:, u:u + 1], mhalf[:], ALU.pow)\
                      .then_inc(rstd_ready[u], 1)

                def scale(t, u, r):
                    pool.wait_ge(stored[u], 16 * r)
                    pool.wait_ge(x_read[u], r + 1)
                    nc.gpsimd.tensor_tensor(x_out[:, u], centred[:, u], g_all[:], ALU.mult).then_inc(scaled[u], 1)

                in_steps(pool, [(0, invert), (1, scale)])

            @block.scalar
            def _(act):
                def store(t, u, r):
                    act.wait_ge(out_ready[u], r + 1)
                    act.dma_start(out[bass.ds(t * P, P), :], x_out[:, u]).then_inc(stored[u], 16)

                in_steps(act, [(0, store)])
                for u in range(2):
                    act.wait_ge(stored[u], 16 * (NT // 2))


def build(nc, x, ln_in_g, ln_in_b, w_in, rpb, lb_fwd, lb_bwd, norm_g, w_na, w_hg, w_out, ln1_g, ln1_b, w_router,
          w_gate, w_up, w_down, ln2_g, ln2_b, out):
    def scratch(name, shape):
        return nc.dram_tensor(name, shape, F32).ap()

    xln, h, aT, o = scratch("xln", [T, D]), scratch("h", [T, IN_W]), scratch("aT", [NAW, T]), scratch("o", [T, HGW])
    mix, x1, y = scratch("mix", [T, D]), scratch("x1", [T, D]), scratch("y", [T, D])
    padded = nc.dram_tensor("padded", [NA_HEADS * (2 * KH - 1), GRID_W, 2 * GRID_W - 1], F32)
    with ExitStack() as ctx:
        s = Stage(nc, ctx, "main")
        ident = s.sb("ident", [P, P])
        stage_consts(nc, ident)
        with ExitStack() as bias:
            b = Stage(nc, bias, "bias")
            table = b.sb("table", [P, NA_HEADS, NROW, GRID_W])
            with ExitStack() as front:
                f = Stage(nc, front, "front")
                xT_hi, xT_lo = f.sb("xT_hi", [P, KD, T], F32R), f.sb("xT_lo", [P, KD, T], F32R)
                stage_norm_in(nc, ident, x, ln_in_g, ln_in_b, xln, xT_hi, xT_lo)
                wide = f.sb("wide", [NA_HEADS * (2 * KH - 1), 2 * GRID_W - 1])
                on_pool = [bias_pad(nc, rpb, padded.ap(), wide, f.sems("pad", 3)),
                           bias_tables(nc, padded, table, f.sems("table", 2))]
                stage_project(nc, w_in, h, xT_hi, xT_lo, on_pool)
            stage_attention(nc, ident, h, table, aT)
        stage_recurrence(nc, ident, h, lb_fwd, lb_bwd, o)
        gates = [s.sb(f"gates{n}", [CAPS[n], NE]) for n in range(2)]
        picks = [s.sb(f"picks{n}", [CAPS[n], NE + 1], U32) for n in range(2)]
        with ExitStack() as routing:
            affT = Stage(nc, routing, "route").sb("affT", [NE, T])
            with ExitStack() as products:
                wraw = [Stage(nc, products, "raw").sb(f"w{n}", [P, NAW // P, D]) for n in range(2)]
                stage_mix(nc, ident, h, aT, o, norm_g, w_na, w_hg, mix, wraw, w_out)
                stage_out(nc, ident, mix, xln, wraw, ln1_g, ln1_b, w_router, x1, y, affT)
            with ExitStack() as experts:
                m = Stage(nc, experts, "pieces")
                ring, w_ready = m.sb("ring", [P, RING, KD * 512]), m.sems("w_ready", RING)

                def load_first_pieces(sp):
                    for n in range(RING):
                        load_piece(sp, ring, w_ready, w_gate, w_up, w_down, 0, n)

                stage_choose(nc, ident, affT, gates, picks, load_first_pieces)
                stage_experts(nc, ident, x1, w_gate, w_up, w_down, gates, picks, y, ring, w_ready)
        stage_norm_out(nc, y, ln2_g, ln2_b, out)


def kernel(**inputs):
    import numpy as np
    import concourse.bacc as bacc
    from concourse import mybir as _mybir
    from concourse.bass_utils import run_bass_kernel_spmd

    arrays = {"x": np.concatenate([np.asarray(inputs["x_prompt"])[0], np.asarray(inputs["x_sample"])[0]], axis=0)}
    for name in ("ln_in_g", "ln_in_b", "w_in", "na_rpb", "hg_lb_fwd", "hg_lb_bwd", "hg_norm_g", "w_branch_na",
                 "w_branch_hg", "w_out", "ln1_g", "ln1_b", "w_router", "w_gate_e", "w_up_e", "w_down_e", "ln2_g",
                 "ln2_b"):
        a = np.asarray(inputs[name])
        if name == "na_rpb":
            arrays[name] = a[0]
        else:
            arrays[name] = a.reshape(-1) if a.size == a.shape[-1] else a.reshape(-1, a.shape[-1])
    nc = bacc.Bacc("TRN2", target_bir_lowering=False, num_devices=1)
    arrays = {f"in_{name}": np.ascontiguousarray(a) for name, a in arrays.items()}
    args = [nc.dram_tensor(name, a.shape, _mybir.dt.from_np(a.dtype), kind="ExternalInput").ap()
            for name, a in arrays.items()]
    args.append(nc.dram_tensor("out", [T, D], _mybir.dt.float32, kind="ExternalOutput").ap())
    build(nc, *args)
    got = run_bass_kernel_spmd(nc, [arrays], core_ids=[0]).results[0]["out"]
    return got[None, 0:SEQS[0][1]], got[None, SEQS[1][0]:]
```
